# Optimizing a Trainium2 kernel written in Bass

```python
import math
import jax, jax.numpy as jnp
from jax import lax
import numpy as np

D_MODEL = 1024
BATCH = 1
SEQ = 1024
DEPTH = 1

D_FF = 2816
CONV_WIDTH = 1024
CONV_HEADS = 16
CONV_K = 3
SSM_WIDTH = 512
SSM_GROUP = 16
SSM_GROUPS = SSM_WIDTH // SSM_GROUP
SSM_STATE = 64
DT_MIN = 0.001
DT_MAX = 0.1
N_MOD = 9
EPS = 1e-6
IN_COLS = 3 * CONV_WIDTH + SSM_WIDTH + 2 * D_MODEL

kernel_name = "hybrid_shortconv_s5_macaron_block"

def rms_norm(x, g):
    xf = x.astype(jnp.float32)
    y = xf * lax.rsqrt(jnp.mean(xf * xf, axis=-1, keepdims=True) + EPS)
    return (y * g.astype(jnp.float32)).astype(x.dtype)

def modulate(h, shift, scale):
    return h * (1.0 + scale[:, None, :]) + shift[:, None, :]

def swiglu(h, w1, w3, w2):
    return (jax.nn.silu(h @ w1) * (h @ w3)) @ w2

def short_conv(v, w):
    return lax.conv_general_dilated(
        v, w[:, None, :].astype(v.dtype), window_strides=(1,),
        padding=((CONV_K - 1, 0),),
        dimension_numbers=("NWC", "WIO", "NWC"),
        feature_group_count=v.shape[-1])

def s5_ssm(u, a_re, a_im, b_re, b_im, c_re, c_im, log_dt):
    bsz, seq, _ = u.shape
    f32 = jnp.float32
    uf = u.astype(f32).reshape(bsz, seq, SSM_GROUPS, SSM_GROUP).transpose(1, 0, 2, 3)
    lam = lax.complex(a_re.astype(f32), a_im.astype(f32))
    dt = jnp.exp(log_dt.astype(f32))[:, None]
    a_bar = jnp.exp(lam * dt)
    b_mat = lax.complex(b_re.astype(f32), b_im.astype(f32))
    b_bar = ((a_bar - 1.0) / lam)[..., None] * b_mat
    c_mat = lax.complex(c_re.astype(f32), c_im.astype(f32))
    bu = jnp.einsum("sbgh,gph->sbgp", uf.astype(jnp.complex64), b_bar)
    a_seq = jnp.broadcast_to(a_bar, (seq, 1) + a_bar.shape)

    def combine(left, right):
        a_l, b_l = left
        a_r, b_r = right
        return (a_r * a_l, a_r * b_l + b_r)

    _, states = lax.associative_scan(combine, (a_seq, bu), axis=0)
    y = jnp.einsum("sbgp,ghp->sbgh", states, c_mat).real
    return y.transpose(1, 0, 2, 3).reshape(bsz, seq, SSM_WIDTH)

def hybrid_mixer(h, w_in, conv_w, w_conv_out, a_re, a_im, b_re, b_im, c_re, c_im,
                 log_dt, d_skip, w_glu, w_ssm_out, w_out):
    proj = h @ w_in
    cuts = [CONV_WIDTH, 2 * CONV_WIDTH, 3 * CONV_WIDTH,
            3 * CONV_WIDTH + SSM_WIDTH, 3 * CONV_WIDTH + SSM_WIDTH + D_MODEL]
    gate_b, gate_c, v, u, glog_a, glog_b = jnp.split(proj, cuts, axis=-1)
    y_a = (gate_b * short_conv(gate_c * v, conv_w)) @ w_conv_out
    s = s5_ssm(u, a_re, a_im, b_re, b_im, c_re, c_im, log_dt).astype(u.dtype) + d_skip * u
    s = jax.nn.gelu(s)
    s = s * jax.nn.sigmoid(s @ w_glu)
    y_b = s @ w_ssm_out
    merged = jax.nn.sigmoid(glog_a) * y_a + jax.nn.sigmoid(glog_b) * y_b
    return merged @ w_out

def setup_inputs(seed: int = 0) -> dict:
    key = jax.random.key(seed)
    ks = jax.random.split(key, 32)
    L, D, G, P, H = DEPTH, D_MODEL, SSM_GROUPS, SSM_STATE, SSM_GROUP
    nrm = lambda k, shape, s: jax.random.normal(k, shape, jnp.float32) * s
    gain = lambda k: 1.0 + 0.02 * jax.random.normal(k, (L, D), jnp.float32)
    a_im_base = jnp.pi * jnp.arange(P, dtype=jnp.float32)
    return {
        "x": nrm(ks[0], (BATCH, SEQ, D), 1.0),
        "c": nrm(ks[1], (BATCH, D), 1.0),
        "w_ada": nrm(ks[2], (L, D, N_MOD * D), 0.5 * D ** -0.5),
        "b_ada": nrm(ks[3], (L, N_MOD * D), 0.01),
        "g_ffn1": gain(ks[4]),
        "w1_a": nrm(ks[5], (L, D, D_FF), D ** -0.5),
        "w3_a": nrm(ks[6], (L, D, D_FF), D ** -0.5),
        "w2_a": nrm(ks[7], (L, D_FF, D), D_FF ** -0.5),
        "g_mix": gain(ks[8]),
        "w_in": nrm(ks[9], (L, D, IN_COLS), D ** -0.5),
        "conv_w": nrm(ks[10], (L, CONV_K, CONV_WIDTH), CONV_K ** -0.5),
        "w_conv_out": nrm(ks[11], (L, CONV_WIDTH, D), CONV_WIDTH ** -0.5),
        "a_re": -0.5 + nrm(ks[12], (L, G, P), 0.01),
        "a_im": a_im_base + nrm(ks[13], (L, G, P), 0.01),
        "b_re": nrm(ks[14], (L, G, P, H), (2.0 * H) ** -0.5),
        "b_im": nrm(ks[15], (L, G, P, H), (2.0 * H) ** -0.5),
        "c_re": nrm(ks[16], (L, G, H, P), P ** -0.5),
        "c_im": nrm(ks[17], (L, G, H, P), P ** -0.5),
        "log_dt": jax.random.uniform(ks[18], (L, G), jnp.float32,
                                     math.log(DT_MIN), math.log(DT_MAX)),
        "d_skip": nrm(ks[19], (L, SSM_WIDTH), 1.0),
        "w_glu": nrm(ks[20], (L, SSM_WIDTH, SSM_WIDTH), SSM_WIDTH ** -0.5),
        "w_ssm_out": nrm(ks[21], (L, SSM_WIDTH, D), SSM_WIDTH ** -0.5),
        "w_out": nrm(ks[22], (L, D, D), D ** -0.5),
        "g_ffn2": gain(ks[23]),
        "w1_b": nrm(ks[24], (L, D, D_FF), D ** -0.5),
        "w3_b": nrm(ks[25], (L, D, D_FF), D ** -0.5),
        "w2_b": nrm(ks[26], (L, D_FF, D), D_FF ** -0.5),
        "g_final": 1.0 + 0.02 * jax.random.normal(ks[27], (D,), jnp.float32),
    }

def reference(x, c, w_ada, b_ada, g_ffn1, w1_a, w3_a, w2_a, g_mix, w_in, conv_w,
              w_conv_out, a_re, a_im, b_re, b_im, c_re, c_im, log_dt, d_skip, w_glu,
              w_ssm_out, w_out, g_ffn2, w1_b, w3_b, w2_b, g_final):
    cond = jax.nn.silu(c)
    for l in range(DEPTH):
        mod = cond @ w_ada[l] + b_ada[l]
        sh1, sc1, gt1, sh2, sc2, gt2, sh3, sc3, gt3 = jnp.split(mod, N_MOD, axis=-1)
        h = modulate(rms_norm(x, g_ffn1[l]), sh1, sc1)
        x = x + 0.5 * gt1[:, None, :] * swiglu(h, w1_a[l], w3_a[l], w2_a[l])
        h = modulate(rms_norm(x, g_mix[l]), sh2, sc2)
        x = x + gt2[:, None, :] * hybrid_mixer(
            h, w_in[l], conv_w[l], w_conv_out[l], a_re[l], a_im[l], b_re[l], b_im[l],
            c_re[l], c_im[l], log_dt[l], d_skip[l], w_glu[l], w_ssm_out[l], w_out[l])
        h = modulate(rms_norm(x, g_ffn2[l]), sh3, sc3)
        x = x + 0.5 * gt3[:, None, :] * swiglu(h, w1_b[l], w3_b[l], w2_b[l])
    return rms_norm(x, g_final)


_drawn_inputs = setup_inputs


def setup_inputs(seed=0):
    import zlib

    import numpy as np

    out = dict(_drawn_inputs(seed))
    spreads = {}
    factors = {'b_ada': 5.455,
     'g_ffn1': 8.0,
     'g_mix': 8.0,
     'a_re': 64.0,
     'a_im': 64.0,
     'b_re': 64.0,
     'b_im': 64.0,
     'c_re': 64.0,
     'c_im': 64.0,
     'log_dt': 64.0,
     'w_glu': 25.608,
     'g_ffn2': 64.0,
     'g_final': 9.717,
     'd_skip': 8.0,
     'w_ssm_out': 7.726}
    for name, (base, spread) in spreads.items():
        noise = np.random.default_rng([zlib.crc32(name.encode()), seed]).standard_normal(out[name].shape)
        drawn = base * np.exp(spread * noise) if base else spread * noise
        out[name] = __import__('jax').numpy.asarray(drawn.astype(out[name].dtype))
    for name, factor in factors.items():
        out[name] = (out[name] * factor).astype(out[name].dtype)
    return out
```

```python
from contextlib import ExitStack

import concourse.bass as bass
from concourse import mybir

F32 = mybir.dt.float32
F32R = mybir.dt.float32r
ACT = mybir.ActivationFunctionType
ALU = mybir.AluOpType

P = 128
D = 1024
T = 1024
KD = D // P
J = 8
C = T // J
FF = 2816
FT = FF // P
CHUNKS = ((0, 8), (8, 8), (16, 6))
G, H, NS = 32, 16, 64
KP = G // 2
NT = G * H // P
LEVELS = 7
PAD = C // 2
NMOD = 9 * KD
EPS = 1e-6
PI = 3.141592653589793
ROUND = 12582912.0
TWO_PI = (6.28125, 0.0019350051879882812, 3.0199159819104966e-07)

A_, B_, C_, D_ = range(4)


def phases():
    out = [("setup", 0, (2, 1, 4, 4), 0, 8)]

    def ffn(name, ada):
        for n, (_, count) in enumerate(CHUNKS):
            c = count if ada and n < 2 else 0
            out.append((f"{name}.up{n}", 2 * count, (count, count, c, 0), count, 0))
            out.append((f"{name}.down{n}", KD, (0, 0, 4, 4), 0, 0))

    ffn("ffn1", True)
    out.append(("norm1", 0, (1, 0, 0, 0), 0, 8))
    out.append(("u", NT, (2, 2, 1, 0), 0, 0))
    out.append(("gates", 16, (8, 8, 8, 8), 0, 0))
    out.append(("conv_in0", 12, (4, 4, 4, 0), 0, 0))
    out.append(("glu", 4, (1, 1, 1, 1), 0, 0))
    out.append(("conv_in1", 12, (4, 4, 4, 0), 0, 0))
    out.append(("ssm_out", 4, (2, 2, 2, 2), 0, 8))
    out.append(("conv_out", KD, (4, 4, 0, 0), 8, 0))
    out.append(("w_out", KD, (0, 0, 4, 4), 0, 0))
    out.append(("norm2", 0, (1, 0, 0, 0), 0, 8))
    ffn("ffn2", False)
    out.append(("end", 0, (0, 0, 0, 0), 0, 0))
    return out


class At:

    def __init__(self, slab, unit, g, h):
        self.slab, self.unit, self.g, self.h = slab, unit, g, h


def starts():
    at, slab, unit, g, h = {}, 0, [0, 0, 0, 0], 0, 0
    for name, slabs, units, gs, hs in phases():
        at[name] = At(slab, tuple(unit), g, h)
        slab, g, h = slab + slabs, g + gs, h + hs
        unit = [a + b for a, b in zip(unit, units)]
    return at


def column(ap, m):
    return ap.rearrange("p (m o) -> p m o", o=1)[:, m, :]


class Steps:

    def __init__(self, engine, semaphore):
        self.engine, self.semaphore, self.base, self.k = engine, semaphore, 0, 0

    def then(self, instruction):
        instruction.then_inc(self.semaphore, 1)
        self.k += 1
        self.engine.wait_ge(self.semaphore, self.base + self.k)

    def enter(self, i, each):
        self.start = self.base + self.k
        self.base, self.k, self.each = self.start + i * each, 0, each

    def leave(self, turns):
        assert self.k == self.each, (self.k, self.each)
        self.base, self.k = self.start + turns * self.each, 0


def block_kernel(nc, a, out):
    at = starts()
    with ExitStack() as ctx:
        base = (nc.sbuf_base + 31) // 32 * 32
        top = [base]

        def region(nbytes):
            at_ = top[0]
            top[0] += nbytes
            return at_

        KB = 1024
        rX, rH, rM, rA = region(32 * KB), region(64 * KB), region(64 * KB), region(16 * KB)
        rRaw, rW, rS = region(16 * KB), region(16 * KB), region(8 * KB)

        def sb(name, shape, offset, dt=F32):
            return nc.alloc_sbuf_tensor_at(name, shape, dt, offset=offset)

        raw = sb("raw", [P, 4, KD, P], rRaw)
        w_high = sb("w_high", [P, 2, KD, P], rW, F32R)
        w_low = sb("w_low", [P, 2, KD, P], rW + 8 * KB, F32R)
        x_res = sb("x_res", [P, KD, T], rX)
        h_high = sb("h_high", [P, KD, T], rH, F32R)
        h_low = sb("h_low", [P, KD, T], rH + 32 * KB, F32R)
        g_high = sb("g_high", [P, KD, T], rM, F32R)
        g_low = sb("g_low", [P, KD, T], rM + 32 * KB, F32R)
        s0 = sb("s0", [P, T], rS)
        s1 = sb("s1", [P, T], rS + 4 * KB)
        stage = (s0, s1)
        x_rows = sb("x_rows", [P, J, D], rH)
        ada_first = sb("ada_first", [P, KD, 16 * P], rM)
        ada_raw = sb("ada_raw", [P, KD, 4 * P], rA)
        rstd = sb("rstd", [P, T], rA)
        xr0 = sb("xr0", [P, T], rA + 4 * KB)
        u_all = sb("u_all", [P, NT, T], rM)
        y_all = sb("y_all", [P, NT, T], rM + 16 * KB)
        s_high = sb("s_high", [P, NT, T], rM + 32 * KB, F32R)
        s_low = sb("s_low", [P, NT, T], rM + 48 * KB, F32R)
        y_chunk = sb("y_chunk", [P, 8, C], rM + 32 * KB)
        c_rows = sb("c_rows", [H, 2, KP, P], rM + 36 * KB)
        ca = sb("ca", [P, 4, 2, 9, H], rX)
        xt = sb("xt", [P, 4, 2, P], rX + 4608)
        toep = sb("toep", [P, 8, P], rX + 8704)
        sc_a = sb("sc_a", [P, 4, 2, PAD + C], rX + 12800)
        sc_b = sb("sc_b", [P, 4, 2, PAD + C], rX + 18944)
        u_chunk = sb("u_chunk", [P, 8, C], rX + 25088)
        ba = sb("ba", [P, 4, 2, J, H], rA)
        k_rows = sb("k_rows", [H, 8, P], rA + 4 * KB)
        b_now = sb("b_now", [P, 4, 2, H], rA + 8 * KB)
        za = sb("za", [P, KD, T], rX)
        gv = sb("gv", [P, J + 2, C], rA)
        taps = sb("taps", [P, T], rA + 5 * KB)
        mb = sb("mb", [P, KD, T], rX)
        merged = sb("merged", [P, T], rA)
        o_rows = sb("o_rows", [P, J, D], rH)
        o_out = sb("o_out", [P, J, D], rH + 32 * KB)
        gf_row = sb("gf_row", [P, D], rA)
        sumsq = sb("sumsq", [P, J], rA + 4 * KB)
        rms = sb("rms", [P, J], rA + 4 * KB + 64)

        def small(name, shape, dt=F32):
            size = 4
            for n in shape[1:]:
                size *= n
            return sb(name, shape, region((size + 31) // 32 * 32), dt)

        ident = small("ident", [P, P])
        ones = small("ones", [P, P])
        v_rows = small("v_rows", [P, P])
        d_rows = small("d_rows", [NT, P])
        vt = small("vt", [P, P + NT])
        cond = small("cond", [P, KD])
        mod = small("mod", [P, NMOD])
        scale = [small(f"scale{n}", [P, KD]) for n in range(3)]
        gate = [small(f"gate{n}", [P, KD]) for n in (0, 2)]
        eps = small("eps", [P, 1])
        lam = sb("lam", [P, 2, KP], rM + 52 * KB)
        dt_ = sb("dt_", [P, KP], rM + 52 * KB + 128)
        q = [sb(f"q{n}", [P, KP], rM + 52 * KB + 192 + 64 * n) for n in range(8)]
        b_in = sb("b_in", [P, 2, KP, H], rM + 53 * KB)
        tmp6 = sb("tmp6", [P, 640], rM + 55 * KB)
        pw = sb("pw", [P, 2, 9, KP], rA + 9 * KB)
        pv = sb("pv", [P, 2, J, KP], rM + 58 * KB)
        lv = sb("lv", [P, LEVELS, 3, KP], rA + 9 * KB + 1152)
        b_bar = sb("b_bar", [P, 2, KP, H], rA + 9 * KB + 2496)
        c_mat = sb("c_mat", [P, 2, KP, H], rA + 9 * KB + 4544)
        assert top[0] <= nc.sbuf_usable_end, top[0]
        B_ADA, GN, CW, DS = 8, (80, 88, 96), 104, P
        SH, SC, GT = (0, 24, 48), (8, 32, 56), (16, 40, 64)

        unit = [ctx.enter_context(nc.psum_tensor(f"unit_{x}", [P, T], F32)) for x in "abcd"]

        x_kept = nc.dram_tensor("x_kept", (P, KD * T), F32).ap()
        u_kept = nc.dram_tensor("u_kept", (NT, P, T), F32).ap()
        y_kept = nc.dram_tensor("y_kept", (NT, P, T), F32).ap()
        sg_kept = nc.dram_tensor("sg_kept", (16, P, T), F32).ap()

        def sem(name):
            return ctx.enter_context(nc.semaphore(name))

        slab_loaded = [sem(f"slab_loaded{r}") for r in range(4)]
        high_split = sem("high_split")
        slab_split = sem("slab_split")
        slab_used = sem("slab_used")
        unit_free = [sem(f"unit_free_{x}") for x in "abcd"]
        rows_loaded = sem("rows_loaded")
        x_loaded = sem("x_loaded")
        ada_loaded = sem("ada_loaded")
        ada_more = sem("ada_more")
        consts = sem("consts")
        setup_full = sem("setup_full")
        vt_ready = sem("vt_ready")
        cond_ready = sem("cond_ready")
        ada_full = sem("ada_full")
        mod_done = sem("mod_done")
        sq_done = sem("sq_done")
        acc_done = sem("acc_done")
        stat_full = sem("stat_full")
        root_done = sem("root_done")
        xr_done = sem("xr_done")
        y_done = sem("y_done")
        h_split = sem("h_split")
        h_ready = sem("h_ready")
        g_split = sem("g_split")
        g_ready = sem("g_ready")
        x_kept_done = sem("x_kept_done")
        lam_loaded = sem("lam_loaded")
        b_loaded = sem("b_loaded")
        u_kept_done = sem("u_kept_done")
        trig = sem("trig")
        trig_act = sem("trig_act")
        ba_ready = sem("ba_ready")
        ssm_full = sem("ssm_full")
        u_loaded = sem("u_loaded")
        toep_loaded = sem("toep_loaded")
        toep_clear = sem("toep_clear")
        scan_step = sem("scan_step")
        scan_done = sem("scan_done")
        sg_saved = [sem("sg_saved0"), sem("sg_saved1")]
        sg_loaded = [sem("sg_loaded0"), sem("sg_loaded1")]
        y_saved = sem("y_saved")
        y_loaded = sem("y_loaded")
        s_sum = sem("s_sum")
        s_split = sem("s_split")
        s_ready = sem("s_ready")
        gated = sem("gated")
        merged_done = sem("merged_done")
        x_back = sem("x_back")
        gf_loaded = sem("gf_loaded")
        out_full = sem("out_full")
        o_final = sem("o_final")
        stored = sem("stored")
        act_step = sem("act_step")
        dve_step = sem("dve_step")

        block = ctx.enter_context(nc.Block())

        @block.sync
        def _(sp):
            def row(dst, src, first):
                n = src.shape[0]
                sp.dma_start(dst[first:first + n, :], src).then_inc(rows_loaded, 16)

            def tiles(ap):
                return ap.rearrange("(m p) -> m p", p=P)

            row(v_rows, tiles(a["c"][0]), 0)
            row(v_rows, tiles(a["b_ada"][0]), B_ADA)
            for n, name in enumerate(("g_ffn1", "g_mix", "g_ffn2")):
                row(v_rows, tiles(a[name][0]), GN[n])
            row(v_rows, a["conv_w"][0].rearrange("k (m p) -> (k m) p", p=P), CW)
            row(d_rows, tiles(a["d_skip"][0]), 0)
            x_tok = a["x"][0].rearrange("(c j) n -> c j n", j=J)
            for j in range(J):
                sp.dma_start(x_rows[:, j, :], x_tok[:, j, :]).then_inc(x_loaded, 16)
            ada = a["w_ada"][0].rearrange("(k p) n -> p k n", p=P)
            for k in range(KD):
                sp.dma_start(ada_first[:, k, :], ada[:, k, 0:16 * P]).then_inc(ada_loaded, 16)

            def load(s, r, src, tiles_k=KD):
                if not (isinstance(s, int) and s < 4):
                    sp.wait_ge(slab_split, s - 3)
                sp.dma_start(raw[:, r, 0:tiles_k, :], src).then_inc(slab_loaded[r], 16)

            def ffn(name, w1, w3, w2, with_ada):
                v1 = w1.rearrange("(k p) (f n) -> p k f n", p=P, n=P)
                v3 = w3.rearrange("(k p) (f n) -> p k f n", p=P, n=P)
                v2 = w2.rearrange("(k p) (m n) -> p k m n", p=P, n=P)
                for n, (f0, count) in enumerate(CHUNKS):
                    here = at[f"{name}.up{n}"].slab
                    many = (4, 3, 0)[n] if with_ada else 0

                    def up(i):
                        for e in range(2):
                            load(here + 4 * i + 2 * e, 2 * e, v1[:, :, f0 + 2 * i + e, :])
                            load(here + 4 * i + 2 * e + 1, 2 * e + 1, v3[:, :, f0 + 2 * i + e, :])
                        if many:
                            first, turn0 = ((16, 0), (48, 8))[n]
                            cols = ada[:, :, first * P:(first + many * count) * P].rearrange(
                                "p k (i m) -> p k i m", m=many * P)
                            if n == 0:
                                sp.wait_ge(h_ready, KD)
                            for e in range(2):
                                sp.wait_ge(ada_full, turn0 + 1 + 2 * i + e)
                                sp.dma_start(ada_raw[:, :, 0:many * P], cols[:, :, 2 * i + e, :]).then_inc(ada_more, 16)

                    up(0)
                    with sp.Fori(1, count // 2) as i:
                        up(i)
                    here2 = at[f"{name}.down{n}"].slab
                    with sp.Fori(0, KD // 4) as i:
                        for r in range(4):
                            load(here2 + 4 * i + r, r, v2[:, f0:f0 + count, 4 * i + r, :], count)

            ffn("ffn1", a["w1_a"][0], a["w3_a"][0], a["w2_a"][0], True)

            w_in = a["w_in"][0].rearrange("(k p) (m n) -> p k m n", p=P, n=P)
            for r in range(NT):
                load(at["u"].slab + r, r, w_in[:, :, 24 + r, :])
            for first, where in ((36, 0), (28, 8)):
                with sp.Fori(0, 2) as i:
                    for r in range(4):
                        load(at["gates"].slab + where + 4 * i + r, r, w_in[:, :, first + 4 * i + r, :])

            def conv_in(name, m0):
                n = 0
                for m in range(m0, m0 + 4):
                    for col in (8, 16, 0):
                        load(at[name].slab + n, n % 4, w_in[:, :, col + m, :])
                        n += 1

            conv_in("conv_in0", 0)
            glu = a["w_glu"][0].rearrange("(k p) (m n) -> p k m n", p=P, n=P)
            for r in range(NT):
                load(at["glu"].slab + r, r, glu[:, :, r, :], NT)
            conv_in("conv_in1", 4)
            w_so = a["w_ssm_out"][0].rearrange("(k p) (m n) -> p k m n", p=P, n=2 * P)
            for r in range(4):
                sp.wait_ge(slab_split, at["ssm_out"].slab + r - 3)
                sp.dma_start(raw[:, r, :, :].rearrange("p (k e) n -> p k (e n)", e=2),
                             w_so[:, :, r, :]).then_inc(slab_loaded[r], 16)
            for name, w in (("conv_out", a["w_conv_out"][0]), ("w_out", a["w_out"][0])):
                v = w.rearrange("(k p) (m n) -> p k m n", p=P, n=P)
                with sp.Fori(0, 2) as i:
                    for r in range(4):
                        load(at[name].slab + 4 * i + r, r, v[:, :, 4 * i + r, :])
            ffn("ffn2", a["w1_b"][0], a["w3_b"][0], a["w2_b"][0], False)
            out_tok = out[0].rearrange("(c j) n -> c j n", j=J)
            for j in range(J):
                sp.wait_ge(o_final, j + 1)
                sp.dma_start(out_tok[:, j, :], o_out[:, j, :]).then_inc(stored, 16)
            sp.wait_ge(stored, 16 * J)

        @block.gpsimd
        def _(pool):
            pool.memset(ident[:, :], 0.0).then_inc(consts, 1)
            pool.memset(ones[:, :], 1.0).then_inc(consts, 1)
            pool.memset(eps[:, :], EPS).then_inc(consts, 1)
            pool.wait_ge(consts, 3)
            pool.affine_select(out=ident[:, :], in_=ident[:, :], compare_op=ALU.not_equal, fill=1.0,
                               base=0, pattern=[[-1, P]], channel_multiplier=1).then_inc(consts, 1)

            one = ones[:, :].rearrange("p (o n) -> p o n", o=1).to_broadcast([P, KD, P])

            def split(i, first):
                for r in range(4):
                    pool.wait_ge(slab_loaded[r], 16 * (i + 1))
                    if not first or r >= 2:
                        pool.wait_ge(slab_used, 4 * i + r - 1)
                    high = w_high[:, r % 2, :, :]
                    pool.tensor_tensor(high, raw[:, r, :, :], one, ALU.mult).then_inc(high_split, 1)
                    pool.wait_ge(high_split, 4 * i + r + 1)
                    pool.tensor_tensor(w_low[:, r % 2, :, :], raw[:, r, :, :], high.bitcast(F32),
                                       ALU.subtract).then_inc(slab_split, 1)

            split(0, True)
            with pool.Fori(1, at["end"].slab // 4) as i:
                split(i, False)

        @block.tensor
        def _(pe):
            def take(u, uses):
                if not (isinstance(uses, int) and uses == 0):
                    pe.wait_ge(unit_free[u], uses)

            def product(u, slot, high, low, kts, cols=slice(0, P), ready=None, row=None):
                for k in range(kts):
                    if ready is not None:
                        pe.wait_ge(ready[0], ready[1] + k + 1)
                    wk = k if row is None else row(k)
                    wh = w_high[:, slot, wk, cols]
                    wl = w_low[:, slot, wk, cols]
                    for part, (w, x) in enumerate(((wh, high), (wh, low), (wl, high))):
                        for half in range(2):
                            t = slice(512 * half, 512 * half + 512)
                            last = pe.matmul(unit[u][:, t], w, x[:, k, t], start=(k == 0 and part == 0),
                                             stop=(k == kts - 1 and part == 2))
                return last

            def slab(s, slot, u, uses, high, low, kts, ready=None):
                pe.wait_ge(slab_split, s + 1)
                take(u, uses)
                product(u, slot, high, low, kts, ready=ready).then_inc(slab_used, 1)

            pe.wait_ge(consts, 4)
            pe.wait_ge(rows_loaded, 7 * 16)
            pe.transpose(unit[A_][:, 0:P], v_rows[:, :], ident[:, :])
            pe.transpose(unit[A_][:, P:P + NT], d_rows[:, :], ident[0:NT, 0:NT]).then_inc(setup_full, 1)
            pe.wait_ge(x_loaded, 16 * J)
            for j in range(J):
                u, uses = (C_, D_)[j % 2], j // 2
                take(u, uses)
                for m in range(KD):
                    last = pe.transpose(unit[u][:, m * P:(m + 1) * P], x_rows[:, j, m * P:(m + 1) * P], ident[:, :])
                last.then_inc(setup_full, 1)

            def ada_tiles(w, count, u):
                for t in range(count):
                    for k in range(KD):
                        last = pe.matmul(unit[u][:, t:t + 1], w[:, k, t * P:(t + 1) * P], cond[:, k:k + 1],
                                         start=(k == 0), stop=(k == KD - 1))
                last.then_inc(ada_full, 1)

            def statistics(n, uses):
                pe.wait_ge(acc_done, KD * (n + 1))
                take(A_, uses)
                for half in range(2):
                    t = slice(512 * half, 512 * half + 512)
                    last = pe.matmul(unit[A_][:, t], ones[:, :], s1[:, t], start=True, stop=True)
                last.then_inc(stat_full, 1)

            pe.wait_ge(cond_ready, 1)
            pe.wait_ge(ada_loaded, 16 * KD)
            ada_tiles(ada_first, 16, B_)
            statistics(0, 1)

            def up(name, n, i, with_ada):
                here = at[f"{name}.up{n}"]
                ready = (h_ready, here.h - KD)
                slab(here.slab + 2 * i, 0, A_, here.unit[A_] + i, h_high, h_low, KD, ready)
                slab(here.slab + 2 * i + 1, 1, B_, here.unit[B_] + i, h_high, h_low, KD)
                if with_ada and n < 2:
                    pe.wait_ge(ada_more, 16 * (8 * n + i + 1))
                    take(C_, here.unit[C_] + i)
                    ada_tiles(ada_raw, 4 - n, C_)

            def down(name, kts, i):
                here = at[name]
                for e in range(2):
                    slab(here.slab + 2 * i + e, e, C_ + e, here.unit[C_ + e] + i, g_high, g_low, kts,
                         (g_ready, here.g - kts))

            def ffn(name, with_ada, last):
                for n, (_, count) in enumerate(CHUNKS):
                    with pe.Fori(0, count) as i:
                        up(name, n, i, with_ada)
                    with pe.Fori(0, KD // 2) as i:
                        down(f"{name}.down{n}", count, i)

            ffn("ffn1", True, False)
            statistics(1, at["norm1"].unit[A_])

            here = at["u"]
            for t in range(NT):
                slab(here.slab + t, t % 2, t % 2, here.unit[t % 2] + t // 2, h_high, h_low, KD, (h_ready, here.h - KD))
            pe.wait_ge(b_loaded, 16 * 4)
            take(C_, here.unit[C_])
            for part in range(2):
                for k in range(KP):
                    col = (part * KP + k) * H
                    last = pe.transpose(unit[C_][:, col:col + H], c_rows[:, part, k, :], ident[0:H, 0:H])
            last.then_inc(ssm_full, 1)

            here = at["gates"]

            def gates(t):
                def gate_slab(q_):
                    slab(here.slab + 4 * t + q_, q_ % 2, q_ % 2, here.unit[q_ % 2] + 2 * t + q_ // 2, h_high, h_low, KD)

                pe.wait_ge(ba_ready, t + 1)
                take(D_, here.unit[D_] + 2 * t)
                take(C_, here.unit[C_] + 2 * t)
                for kk in range(4):
                    for part in range(2):
                        col = (2 * kk + part) * P
                        last = pe.transpose(unit[C_][:, col:col + P],
                                            ba[:, kk, part, :, :].rearrange("p j h -> p (j h)"), ident[:, :])
                last.then_inc(ssm_full, 1)
                for g2 in range(2):
                    rows = slice(NS * g2, NS * g2 + NS)
                    for kk in range(4):
                        col = (4 * g2 + kk) * P
                        for part in range(2):
                            last = pe.matmul(unit[D_][0:H, col:col + P], b_now[rows, kk, part, :],
                                             ca[rows, kk, part, 0:8, :].rearrange("p d h -> p (d h)"),
                                             start=(part == 0), stop=(part == 1))
                last.then_inc(ssm_full, 1)
                gate_slab(0)
                pe.wait_ge(unit_free[C_], here.unit[C_] + 2 * t + 1)
                pe.wait_ge(u_loaded, 128 * (t + 1))
                for g2 in range(2):
                    for kk in range(4):
                        for part in range(2):
                            col = (2 * kk + part) * P
                            last = pe.matmul(unit[C_][NS * g2:NS * g2 + NS, col:col + P],
                                             xt[:, kk, part, NS * g2:NS * g2 + NS], u_chunk[:, 2 * kk + g2, :],
                                             start=True, stop=True)
                last.then_inc(ssm_full, 1)
                gate_slab(1)
                gate_slab(2)
                pe.wait_ge(scan_done, t + 1)
                pe.wait_ge(toep_loaded, 128 * (t + 1))
                take(D_, here.unit[D_] + 2 * t + 1)
                for g2 in range(2):
                    rows = slice(NS * g2, NS * g2 + NS)
                    for kk in range(4):
                        dst = unit[D_][:, (4 * g2 + kk) * P:(4 * g2 + kk + 1) * P]
                        pe.matmul(dst, toep[:, 4 * g2 + kk, :], u_chunk[:, 2 * kk + g2, :], start=True, stop=False)
                        for part in range(2):
                            last = pe.matmul(dst, ca[rows, kk, part, 1:9, :].rearrange("p d h -> p (d h)"),
                                             sc_b[rows, kk, part, PAD:], start=False, stop=(part == 1))
                last.then_inc(ssm_full, 1)
                gate_slab(3)

            with pe.Fori(0, NT) as t:
                gates(t)

            def conv_in(name):
                here = at[name]
                with pe.Fori(0, 2) as i:
                    for e in range(2):
                        for n, u in enumerate((A_, B_, C_)):
                            slab(here.slab + 6 * i + 3 * e + n, (3 * e + n) % 2, u, here.unit[u] + 2 * i + e,
                                 h_high, h_low, KD)

            conv_in("conv_in0")
            here = at["glu"]
            for t in range(NT):
                slab(here.slab + t, t % 2, t, here.unit[t], s_high, s_low, NT, (s_ready, 0))
            conv_in("conv_in1")
            here = at["ssm_out"]
            with pe.Fori(0, 2) as i:
                for e in range(2):
                    pe.wait_ge(slab_split, here.slab + 2 * i + e + 1)
                    for half in range(2):
                        u = 2 * e + half
                        take(u, here.unit[u] + i)
                        last = product(u, e, s_high, s_low, NT, ready=(s_ready, NT), row=lambda k: 2 * k + half)
                    last.then_inc(slab_used, 1)
            here = at["conv_out"]
            with pe.Fori(0, KD // 2) as i:
                for e in range(2):
                    slab(here.slab + 2 * i + e, e, e, here.unit[e] + i, h_high, h_low, KD, (h_ready, here.h - KD))
            with pe.Fori(0, KD // 2) as i:
                down("w_out", KD, i)
            statistics(2, at["norm2"].unit[A_])
            ffn("ffn2", False, True)

            last_down = at["ffn2.down2"]
            ends = at["end"]
            for m in range(KD):
                pe.wait_ge(unit_free[C_ + m % 2], last_down.unit[C_ + m % 2] + m // 2 + 1)
                take(m % 2, ends.unit[m % 2] + m // 2)
                for j in range(J):
                    last = pe.transpose(unit[m % 2][:, j * P:(j + 1) * P], x_res[:, m, j * P:(j + 1) * P], ident[:, :])
                last.then_inc(out_full, 1)

        @block.scalar
        def _(act):
            own = Steps(act, act_step)

            act.wait_ge(vt_ready, 1)
            act.activation(cond[:, :], vt[:, 0:KD], ACT.Silu).then_inc(cond_ready, 1)
            for j in range(1, J, 2):
                act.wait_ge(setup_full, 2 + j)
                act.activation(x_res[:, :, j * C:(j + 1) * C], unit[D_][:, :].rearrange("p (m c) -> p m c", c=C),
                               ACT.Copy).then_inc(unit_free[D_], 1)

            def square(n, m, first=False):
                if not first:
                    act.wait_ge(acc_done, KD * n + m)
                act.activation(s0[:, :], x_res[:, m, :], ACT.Square).then_inc(sq_done, 1)

            act.wait_ge(unit_free[C_], 4)
            act.wait_ge(unit_free[D_], 4)
            square(0, 0, True)
            with act.Fori(1, KD) as m:
                square(0, m)

            def norm(n, h0):
                act.wait_ge(stat_full, n + 1)
                act.activation(s0[:, :], unit[A_][:, :], ACT.Sqrt, bias=eps[:, 0:1], scale=1.0 / D).then_inc(root_done, 1)

                if n == 1:
                    act.dma_start(x_kept, x_res[:, :, :].rearrange("p k t -> p (k t)")).then_inc(x_kept_done, 16)

                def tile(i):
                    for e in range(2):
                        m = 2 * i + e
                        xr = (xr0, s0)[e]
                        act.wait_ge(xr_done, KD * n + m + 1)
                        own.then(act.activation(xr[:, :], xr[:, :], ACT.Identity, scale=column(scale[n][:, :], m),
                                                bias=column(mod[:, SH[n]:SH[n] + KD], m)))
                        act.activation(h_high[:, m, :], xr[:, :], ACT.Copy).then_inc(h_split, 1)

                with act.Fori(0, KD // 2) as i:
                    own.enter(i, 2)
                    tile(i)
                own.leave(KD // 2)

            norm(0, 0)

            def up(name, n):
                here = at[f"{name}.up{n}"]
                with act.Fori(0, CHUNKS[n][1]) as i:
                    act.wait_ge(slab_used, here.slab + 2 * i + 1)
                    act.activation(s0[:, :], unit[A_][:, :], ACT.Silu).then_inc(unit_free[A_], 1)
                    act.wait_ge(unit_free[B_], here.unit[B_] + i + 1)
                    act.activation(g_high[:, i, :], s1[:, :], ACT.Copy).then_inc(g_split, 1)

            def down_squares(name, n):
                here = at[name]
                with act.Fori(0, KD // 2) as i:
                    for e in range(2):
                        act.wait_ge(unit_free[C_ + e], here.unit[C_ + e] + i + 1)
                        square(n, 2 * i + e)

            for n in range(3):
                up("ffn1", n)
            down_squares("ffn1.down2", 1)
            norm(1, 8)

            def as_states(ap):
                return ap.rearrange("(k g) p -> (g p) k", g=2)

            with nc.allow_non_contiguous_dma(reason="small parameter tables"):
                act.dma_start(lam[:, 0, :], as_states(a["a_re"][0])).then_inc(lam_loaded, 16)
                act.dma_start(lam[:, 1, :], as_states(a["a_im"][0])).then_inc(lam_loaded, 16)
                for g2 in range(2):
                    per = a["log_dt"][0].rearrange("(k g) -> g k", g=2)[g2:g2 + 1, :]
                    act.dma_start(dt_[NS * g2:NS * g2 + NS, :], per.to_broadcast([NS, KP])).then_inc(lam_loaded, 16)
                for part, (b, c) in enumerate((("b_re", "c_re"), ("b_im", "c_im"))):
                    act.dma_start(b_in[:, part, :, :], a[b][0].rearrange("(k g) p h -> (g p) k h", g=2)).then_inc(b_loaded, 16)
                    act.dma_start(c_rows[:, part, :, :].rearrange("h k (g p) -> h (k g) p", g=2),
                                  a[c][0].rearrange("g h p -> h g p")).then_inc(b_loaded, 16)
            act.wait_ge(lam_loaded, 64)
            act.activation(dt_[:, :], dt_[:, :], ACT.Exp).then_inc(trig_act, 1)
            act.wait_ge(trig, 1)
            act.activation(q[3][:, :], q[0][:, :], ACT.Exp).then_inc(trig_act, 1)
            act.wait_ge(trig, 2)
            act.activation(q[4][:, :], q[1][:, :], ACT.Sin).then_inc(trig_act, 1)
            act.activation(q[5][:, :], q[2][:, :], ACT.Sin).then_inc(trig_act, 1)

            here = at["u"]
            for t in range(NT):
                act.wait_ge(slab_used, here.slab + t + 1)
                act.activation(u_all[:, t, :], unit[t % 2][:, :], ACT.Copy).then_inc(unit_free[t % 2], 1)
                act.wait_ge(unit_free[t % 2], here.unit[t % 2] + t // 2 + 1)
                act.dma_start(u_kept[t], u_all[:, t, :]).then_inc(u_kept_done, 16)
            act.wait_ge(u_kept_done, 16 * NT)

            here = at["gates"]

            def gates(t, first):
                def gate_slab(q_):
                    act.wait_ge(slab_used, here.slab + 4 * t + q_ + 1)
                    if not first or q_ >= 2:
                        act.wait_ge(sg_saved[q_ % 2], 16 * (2 * t + q_ // 2))
                    act.activation(stage[q_ % 2][:, :], unit[q_ % 2][:, :], ACT.Sigmoid).then_inc(unit_free[q_ % 2], 1)
                    act.wait_ge(unit_free[q_ % 2], here.unit[q_ % 2] + 2 * t + q_ // 2 + 1)
                    act.dma_start(sg_kept.rearrange("(t q) p n -> q t p n", q=4)[q_][t], stage[q_ % 2][:, :]).then_inc(sg_saved[q_ % 2], 16)

                act.wait_ge(ssm_full, 1 + 4 * t)
                u_src = u_kept.rearrange("t (g h) (j c) -> j t h g c", h=H, j=J)
                for j in range(J):
                    act.dma_start(u_chunk[H * j:H * j + H, :, :], u_src[j][t]).then_inc(u_loaded, 16)
                act.wait_ge(ssm_full, 2 + 4 * t)
                act.activation(xt[:, :, :, :].rearrange("p a b n -> p (a b n)"), unit[C_][:, :], ACT.Copy).then_inc(unit_free[C_], 1)
                act.wait_ge(ssm_full, 3 + 4 * t)
                act.activation(k_rows[:, :, :].rearrange("h g n -> h (g n)"), unit[D_][0:H, :], ACT.Copy).then_inc(unit_free[D_], 1)
                act.wait_ge(unit_free[D_], here.unit[D_] + 2 * t + 1)
                if first:
                    act.wait_ge(toep_clear, 1)
                for j in range(J):
                    act.dma_start(toep[H * j:H * j + H, :, H * j:P], k_rows[:, :, 0:P - H * j]).then_inc(toep_loaded, 16)
                gate_slab(0)
                gate_slab(1)
                gate_slab(2)
                act.wait_ge(ssm_full, 5 + 4 * t)
                act.activation(y_chunk[:, :, :].rearrange("p g c -> p (g c)"), unit[D_][:, :], ACT.Copy).then_inc(unit_free[D_], 1)
                act.wait_ge(unit_free[D_], here.unit[D_] + 2 * t + 2)
                y_dst = y_kept.rearrange("t (k g h) (i c) -> i g t h k c", g=2, h=H, i=J)
                for i in range(J):
                    for g2 in range(2):
                        act.dma_start(y_dst[i][g2][t], y_chunk[H * i:H * i + H, 4 * g2:4 * g2 + 4, :]).then_inc(y_saved, 16)
                gate_slab(3)
                act.wait_ge(y_saved, 256 * (t + 1))
                act.dma_start(y_all[:, t, :], y_kept[t]).then_inc(y_loaded, 16)

            gates(0, True)
            with act.Fori(1, NT) as t:
                gates(t, False)

            for t in range(NT):
                act.wait_ge(s_sum, t + 1)
                own.then(act.activation(u_all[:, t, :], u_all[:, t, :], ACT.Gelu_apprx_tanh))
                act.activation(s_high[:, t, :], u_all[:, t, :], ACT.Copy).then_inc(s_split, 1)

            def conv_in(name):
                here = at[name]
                with act.Fori(0, 4) as m:
                    act.wait_ge(slab_used, here.slab + 3 * m + 1)
                    act.wait_ge(unit_free[B_], here.unit[B_] + m)
                    act.activation(s0[:, :], unit[A_][:, :], ACT.Copy).then_inc(unit_free[A_], 1)

            for stage_ in range(2):
                act.wait_ge(sg_saved[stage_], 16 * 8)
            conv_in("conv_in0")
            here = at["glu"]
            for t in range(NT):
                act.wait_ge(slab_used, here.slab + t + 1)
                if t >= 2:
                    act.wait_ge(gated, t - 1)
                else:
                    act.wait_ge(unit_free[B_], here.unit[B_])
                act.activation(stage[t % 2][:, :], unit[t][:, :], ACT.Sigmoid).then_inc(unit_free[t], 1)
            for t in range(NT):
                act.wait_ge(gated, t + 1)
                act.activation(s_high[:, t, :], u_all[:, t, :], ACT.Copy).then_inc(s_split, 1)
            conv_in("conv_in1")

            def sg_load(n, e):
                act.dma_start(stage[e][:, :], sg_kept[n]).then_inc(sg_loaded[e], 16)

            here = at["ssm_out"]
            act.wait_ge(unit_free[B_], here.unit[B_])
            act.wait_ge(unit_free[C_], here.unit[C_])
            sg_load(0, 0)
            sg_load(1, 1)
            act.wait_ge(slab_used, here.slab)
            with act.Fori(0, 2) as i:
                for u in range(4):
                    m = 4 * i + u
                    act.activation(h_high[:, m, :], za[:, m, :], ACT.Copy).then_inc(h_split, 1)
                    act.wait_ge(unit_free[u], here.unit[u] + i + 1)
                    sg_load(m + 2, u % 2)
            here = at["conv_out"]
            x_tiles = x_kept.rearrange("p (k t) -> k p t", k=KD)
            with nc.allow_non_contiguous_dma(reason="rows of 4 KiB"):
                def conv_out(i, more):
                    for e in range(2):
                        m = 2 * i + e
                        act.wait_ge(unit_free[e], here.unit[e] + i + 1)
                        if more:
                            sg_load(m + 10, e)
                        act.wait_ge(merged_done, m + 1)
                        act.activation(g_high[:, m, :], merged[:, :], ACT.Copy).then_inc(g_split, 1)
                        act.dma_start(x_res[:, m, :], x_tiles[m]).then_inc(x_back, 16)

                with act.Fori(0, KD // 2 - 1) as i:
                    conv_out(i, True)
                conv_out(KD // 2 - 1, False)
            down_squares("w_out", 2)
            norm(2, 24)
            for n in range(3):
                up("ffn2", n)
            act.dma_start(gf_row[:, :], a["g_final"].rearrange("(o n) -> o n", o=1).to_broadcast([P, D])).then_inc(gf_loaded, 16)
            ends = at["end"]
            for m in range(1, KD, 2):
                act.wait_ge(out_full, m + 1)
                act.activation(o_rows[:, :, m * P:(m + 1) * P], unit[B_][:, :].rearrange("p (j n) -> p j n", n=P),
                               ACT.Copy).then_inc(unit_free[B_], 1)
            act.wait_ge(unit_free[A_], ends.unit[A_] + 4)
            act.wait_ge(unit_free[B_], ends.unit[B_] + 4)
            for j in range(J):
                own.then(act.activation(o_out[:, j, :], o_rows[:, j, :], ACT.Square, accum_out=sumsq[:, j:j + 1]))
            act.activation(rms[:, :], sumsq[:, :], ACT.Sqrt, bias=eps[:, 0:1], scale=1.0 / D).then_inc(root_done, 1)

        @block.vector
        def _(dve):
            own = Steps(dve, dve_step)
            mul, add, sub = ALU.mult, ALU.add, ALU.subtract

            dve.wait_ge(setup_full, 1)
            dve.tensor_copy(vt[:, :], unit[A_][:, 0:P + NT]).then_inc(vt_ready, 1)
            dve.wait_ge(vt_ready, 1)
            dve.sem_inc(unit_free[A_], 1)
            for j in range(0, J, 2):
                dve.wait_ge(setup_full, 2 + j)
                dve.tensor_copy(x_res[:, :, j * C:(j + 1) * C],
                                unit[C_][:, :].rearrange("p (m c) -> p m c", c=C)).then_inc(unit_free[C_], 1)

            def accumulate(n, m):
                dve.wait_ge(sq_done, KD * n + m + 1)
                dve.tensor_tensor(s1[:, :], s1[:, :], s0[:, :], add).then_inc(acc_done, 1)
                dve.wait_ge(acc_done, KD * n + m + 1)

            own.then(dve.memset(s1[:, :], 0.0))
            with dve.Fori(0, KD) as m:
                accumulate(0, m)

            dve.wait_ge(ada_full, 1)
            dve.tensor_tensor(mod[:, 0:16], unit[B_][:, 0:16], vt[:, B_ADA:B_ADA + 16], add).then_inc(unit_free[B_], 1)
            dve.wait_ge(unit_free[B_], 1)

            def derive_scale(n):
                return dve.scalar_tensor_tensor(out=scale[n][:, :], in0=mod[:, SC[n]:SC[n] + KD], scalar=1.0,
                                                in1=vt[:, GN[n]:GN[n] + KD], op0=add, op1=mul)

            own.then(derive_scale(0))

            def norm(n, h0, unit_a):
                dve.wait_ge(root_done, n + 1)
                own.then(dve.reciprocal(rstd[:, :], s0[:, :]))
                dve.sem_inc(unit_free[A_], 1)

                def scaled(m, e):
                    dve.tensor_tensor((xr0, s0)[e][:, :], x_res[:, m, :], rstd[:, :], mul).then_inc(xr_done, 1)

                def low(m, e):
                    dve.wait_ge(h_split, h0 + m + 1)
                    dve.tensor_tensor(h_low[:, m, :], (xr0, s0)[e][:, :], h_high[:, m, :].bitcast(F32),
                                      sub).then_inc(h_ready, 1)

                scaled(0, 0)
                scaled(1, 1)
                with dve.Fori(0, KD // 2 - 1) as i:
                    for e in range(2):
                        low(2 * i + e, e)
                        dve.wait_ge(h_ready, h0 + 2 * i + e + 1)
                        scaled(2 * i + e + 2, e)
                low(KD - 2, 0)
                low(KD - 1, 1)
                dve.wait_ge(h_ready, h0 + KD)

            norm(0, 0, 1)

            def up(name, n, with_ada):
                here = at[f"{name}.up{n}"]
                with dve.Fori(0, CHUNKS[n][1]) as i:
                    dve.wait_ge(unit_free[A_], here.unit[A_] + i + 1)
                    dve.wait_ge(slab_used, here.slab + 2 * i + 2)
                    dve.tensor_tensor(s1[:, :], s0[:, :], unit[B_][:, :], mul).then_inc(unit_free[B_], 1)
                    dve.wait_ge(g_split, here.g + i + 1)
                    dve.tensor_tensor(g_low[:, i, :], s1[:, :], g_high[:, i, :].bitcast(F32), sub).then_inc(g_ready, 1)
                    dve.wait_ge(g_ready, here.g + i + 1)
                    if with_ada and n < 2:
                        first, many = ((16, 4), (48, 3))[n]
                        cols = slice(first, first + 8 * many)
                        dve.wait_ge(ada_full, 8 * n + i + 2)
                        dve.tensor_tensor(
                            mod[:, cols].rearrange("p (i t) -> p i t", t=many)[:, i, :], unit[C_][:, 0:many],
                            vt[:, B_ADA + first:B_ADA + first + 8 * many].rearrange("p (i t) -> p i t", t=many)[:, i, :],
                            add).then_inc(unit_free[C_], 1)

            def down(name, g, squares=None):
                here = at[name]
                with dve.Fori(0, KD // 2) as i:
                    for e in range(2):
                        m = 2 * i + e
                        dve.wait_ge(slab_used, here.slab + m + 1)
                        dve.scalar_tensor_tensor(out=x_res[:, m, :], in0=unit[C_ + e][:, :], scalar=column(g, m),
                                                 in1=x_res[:, m, :], op0=mul, op1=add).then_inc(unit_free[C_ + e], 1)
                        if squares is not None:
                            accumulate(squares, m)

            def half_gate(n, k):
                return dve.tensor_scalar(gate[k][:, :], mod[:, GT[n]:GT[n] + KD], 0.5, None, mul)

            up("ffn1", 0, True)
            dve.wait_ge(unit_free[C_], at["ffn1.down0"].unit[C_])
            own.then(half_gate(0, 0))
            down("ffn1.down0", gate[0][:, :])
            up("ffn1", 1, True)
            dve.wait_ge(unit_free[C_], at["ffn1.down1"].unit[C_])
            own.then(derive_scale(1))
            own.then(derive_scale(2))
            own.then(half_gate(2, 1))
            down("ffn1.down1", gate[0][:, :])
            up("ffn1", 2, False)
            dve.wait_ge(g_ready, at["ffn1.down2"].g)
            own.then(dve.memset(s1[:, :], 0.0))
            down("ffn1.down2", gate[0][:, :], 1)
            norm(1, at["norm1"].h, at["norm1"].unit[A_])

            lr, li = lam[:, 0, :], lam[:, 1, :]
            Q = [x[:, :] for x in q]

            def tt(out_, x, y, op):
                own.then(dve.tensor_tensor(out_, x, y, op))

            def ts(out_, x, c0, c1, op0, op1=None):
                if op1 is None:
                    own.then(dve.tensor_scalar(out_, x, c0, None, op0))
                else:
                    own.then(dve.tensor_scalar(out_, x, c0, c1, op0, op1))

            dve.wait_ge(trig_act, 1)
            dve.tensor_tensor(Q[0], lr, dt_[:, :], mul).then_inc(trig, 1)
            tt(Q[1], li, dt_[:, :], mul)
            ts(Q[2], Q[1], 1.0 / (2 * PI), ROUND, mul, add)
            ts(Q[2], Q[2], ROUND, None, sub)
            for part in TWO_PI:
                own.then(dve.scalar_tensor_tensor(out=Q[1], in0=Q[2], scalar=-part, in1=Q[1], op0=mul, op1=add))
            ts(Q[1], Q[1], 3.1415925, -3.1415925, ALU.min, ALU.max)
            ts(Q[6], Q[1], -1.0, None, mul)
            tt(Q[6], Q[6], Q[1], ALU.max)
            dve.tensor_scalar(Q[2], Q[6], -1.0, PI / 2, mul, add).then_inc(trig, 1)
            dve.wait_ge(trig_act, 4)
            tt(pw[:, 0, 1, :], Q[3], Q[5], mul)
            tt(pw[:, 1, 1, :], Q[3], Q[4], mul)
            own.then(dve.memset(pw[:, 0, 0, :], 1.0))
            own.then(dve.memset(pw[:, 1, 0, :], 0.0))

            def cmul(dst, x, y, t0, t1):
                tt(t0, x[0], y[0], mul)
                tt(t1, x[1], y[1], mul)
                tt(dst[0], t0, t1, sub)
                tt(t0, x[0], y[1], mul)
                tt(t1, x[1], y[0], mul)
                tt(dst[1], t0, t1, add)

            for half in (1, 2, 4):
                src = [pw[:, part, 1:half + 1, :] for part in range(2)]
                by = [pw[:, part, half:half + 1, :].to_broadcast([P, half, KP]) for part in range(2)]
                dst = [pw[:, part, half + 1:2 * half + 1, :] for part in range(2)]
                t0, t1 = (tmp6[:, 64 * x:64 * x + half * KP].rearrange("p (d k) -> p d k", k=KP) for x in range(2))
                cmul(dst, src, by, t0, t1)
            for j in range(J):
                own.then(dve.tensor_copy(pv[:, :, j, :], pw[:, :, J - 1 - j, :]))
            for l in range(LEVELS):
                if l == 0:
                    for part in range(2):
                        own.then(dve.tensor_copy(lv[:, 0, part, :], pw[:, part, 8, :]))
                else:
                    prev = [lv[:, l - 1, part, :] for part in range(2)]
                    cmul([lv[:, l, part, :] for part in range(2)], prev, prev, Q[6], Q[7])
            ts(lv[:, :, 2, :], lv[:, :, 1, :], -1.0, None, mul)
            tt(Q[0], lr, lr, mul)
            tt(Q[1], li, li, mul)
            tt(Q[0], Q[0], Q[1], add)
            own.then(dve.reciprocal(Q[0], Q[0]))
            ts(Q[1], pw[:, 0, 1, :], 1.0, None, sub)
            ai = pw[:, 1, 1, :]
            tt(Q[2], Q[1], lr, mul)
            tt(Q[3], ai, li, mul)
            tt(Q[2], Q[2], Q[3], add)
            tt(Q[2], Q[2], Q[0], mul)
            tt(Q[3], ai, lr, mul)
            tt(Q[4], Q[1], li, mul)
            tt(Q[3], Q[3], Q[4], sub)
            tt(Q[3], Q[3], Q[0], mul)
            dve.wait_ge(b_loaded, 64)
            wide = [x.rearrange("p (k o) -> p k o", o=1).to_broadcast([P, KP, H]) for x in (Q[2], Q[3])]
            t0, t1 = (tmp6[:, 256 * x:256 * x + 256].rearrange("p (k h) -> p k h", h=H) for x in range(2))
            cmul([b_bar[:, part, :, :] for part in range(2)], [b_in[:, part, :, :] for part in range(2)], wide, t0, t1)
            dve.wait_ge(x_kept_done, 16)
            own.then(dve.memset(sc_a[:, :, :, :], 0.0))
            own.then(dve.memset(sc_b[:, :, :, :], 0.0))
            dve.memset(toep[:, :, :], 0.0).then_inc(toep_clear, 1)
            dve.wait_ge(ssm_full, 1)
            own.then(dve.tensor_copy(c_mat[:, :, :, :].rearrange("p r k h -> p (r k h)"), unit[C_][:, 0:2 * KP * H]))
            dve.sem_inc(unit_free[C_], 1)

            def batch(t):
                dve.wait_ge(ssm_full, 1 + 4 * t)
                four = "p d (t k) -> p t k d"
                powers = [pw[:, part, :, :].rearrange(four, k=4)[:, t, :, :] for part in range(2)]
                late = [pv[:, part, :, :].rearrange(four, k=4)[:, t, :, :] for part in range(2)]
                bb = [b_bar[:, part, :, :].rearrange("p (t k) h -> p t k h", k=4)[:, t, :, :] for part in range(2)]
                cc = [c_mat[:, part, :, :].rearrange("p (t k) h -> p t k h", k=4)[:, t, :, :] for part in range(2)]
                for part in range(2):
                    own.then(dve.tensor_copy(b_now[:, :, part, :], bb[part]))
                for kk in range(4):
                    def spread(x, n):
                        return x.rearrange("p (d o) -> p d o", o=1).to_broadcast([P, n, H])

                    def over(x, n):
                        return x.rearrange("p (o h) -> p o h", o=1).to_broadcast([P, n, H])

                    pr, pi = (spread(x[:, kk, :], 9) for x in powers)
                    cr, ci = (over(x[:, kk, :], 9) for x in cc)
                    t0, t1 = (tmp6[:, 320 * x:320 * x + 144].rearrange("p (d h) -> p d h", h=H) for x in range(2))
                    own2(dve.tensor_tensor(t0, pr, cr, mul))
                    own.then(dve.tensor_tensor(t1, pi, ci, mul))
                    tt(ca[:, kk, 0, :, :], t0, t1, sub)
                    own2(dve.tensor_tensor(t0, pr, ci, mul))
                    own.then(dve.tensor_tensor(t1, pi, cr, mul))
                    own.then(dve.scalar_tensor_tensor(out=ca[:, kk, 1, :, :], in0=t0, scalar=-1.0, in1=t1,
                                                      op0=mul, op1=sub))
                    pr, pi = (spread(x[:, kk, :], 8) for x in late)
                    br, bi = (over(x[:, kk, :], 8) for x in bb)
                    t0, t1 = (tmp6[:, 320 * x:320 * x + 128].rearrange("p (d h) -> p d h", h=H) for x in range(2))
                    own2(dve.tensor_tensor(t0, pr, br, mul))
                    own.then(dve.tensor_tensor(t1, pi, bi, mul))
                    tt(ba[:, kk, 0, :, :], t0, t1, sub)
                    own2(dve.tensor_tensor(t0, pr, bi, mul))
                    own.then(dve.tensor_tensor(t1, pi, br, mul))
                    tt(ba[:, kk, 1, :, :], t0, t1, add)
                dve.sem_inc(ba_ready, 1)

                dve.wait_ge(ssm_full, 4 + 4 * t)
                own.then(dve.tensor_copy(
                    sc_a[:, :, :, PAD + 1:PAD + C].rearrange("p k r c -> p (k r) c"),
                    unit[C_][:, :].rearrange("p (n c) -> p n c", c=C)[:, :, 0:C - 1]))
                dve.sem_inc(unit_free[C_], 1)
                n = 0
                for pair in range(2):
                    for l in range(LEVELS):
                        src, dst = ((sc_a, sc_b), (sc_b, sc_a))[l % 2]
                        off = 1 << l
                        now, then = slice(PAD, PAD + C), slice(PAD - off, PAD + C - off)
                        for to, from_, x, plus in ((0, 0, 0, src), (1, 1, 0, src), (0, 1, 2, dst), (1, 0, 1, dst)):
                            for kk in (2 * pair, 2 * pair + 1):
                                by = lv[:, l, x, :].rearrange("p (t k) -> p t k", k=4)[:, t, kk:kk + 1]
                                if n >= 2:
                                    dve.wait_ge(scan_step, 4 * 4 * LEVELS * t + n - 1)
                                dve.scalar_tensor_tensor(
                                    out=dst[:, kk, to, now], in0=src[:, kk, from_, then], scalar=by,
                                    in1=plus[:, kk, to, now], op0=mul, op1=add).then_inc(scan_step, 1)
                                n += 1
                dve.wait_ge(scan_step, 4 * 4 * LEVELS * (t + 1))
                dve.sem_inc(scan_done, 1)

            def own2(ins):
                own.then(ins)

            with dve.Fori(0, NT) as t:
                own.enter(t, 2 + 4 * 12 + 1)
                batch(t)
            own.leave(NT)

            dve.wait_ge(y_loaded, 16 * NT)
            for t in range(NT):
                dve.scalar_tensor_tensor(out=u_all[:, t, :], in0=u_all[:, t, :], scalar=vt[:, DS + t:DS + t + 1],
                                         in1=y_all[:, t, :], op0=mul, op1=add).then_inc(s_sum, 1)

            def s_low_part(t, before):
                dve.wait_ge(s_split, before + t + 1)
                dve.tensor_tensor(s_low[:, t, :], u_all[:, t, :], s_high[:, t, :].bitcast(F32), sub).then_inc(s_ready, 1)

            for t in range(NT):
                s_low_part(t, 0)
            own.then(dve.memset(gv[:, 0:2, 0:1], 0.0))

            def conv_in(name, m0):
                here = at[name]
                with dve.Fori(0, 4) as m:
                    own.enter(m, 4)
                    dve.wait_ge(unit_free[A_], here.unit[A_] + m + 1)
                    dve.wait_ge(slab_used, here.slab + 3 * m + 2)
                    dve.tensor_tensor(gv[:, 2:, :].rearrange("p j c -> p (j c)"), s0[:, :], unit[B_][:, :],
                                      mul).then_inc(unit_free[B_], 1)
                    dve.wait_ge(unit_free[B_], here.unit[B_] + m + 1)
                    own.then(dve.tensor_copy(gv[:, 0:2, 1:C], gv[:, J:J + 2, 0:C - 1]))

                    def tap(k):
                        return column(vt[:, CW + k * KD + m0:CW + k * KD + m0 + 4], m)

                    def steps(j):
                        return gv[:, j:j + J, :].rearrange("p j c -> p (j c)")

                    own.then(dve.tensor_scalar(taps[:, :], steps(2), tap(2), None, mul))
                    for k in (1, 0):
                        own.then(dve.scalar_tensor_tensor(out=taps[:, :], in0=steps(k), scalar=tap(k),
                                                          in1=taps[:, :], op0=mul, op1=add))
                    dve.wait_ge(slab_used, here.slab + 3 * m + 3)
                    dve.tensor_tensor(za[:, m0:m0 + 4, :][:, m, :], taps[:, :], unit[C_][:, :],
                                      mul).then_inc(unit_free[C_], 1)
                    dve.wait_ge(unit_free[C_], here.unit[C_] + m + 1)
                own.leave(4)

            conv_in("conv_in0", 0)
            here = at["glu"]
            for t in range(NT):
                dve.wait_ge(unit_free[t], here.unit[t] + 1)
                dve.tensor_tensor(u_all[:, t, :], u_all[:, t, :], stage[t % 2][:, :], mul).then_inc(gated, 1)
            for t in range(NT):
                s_low_part(t, NT)
            conv_in("conv_in1", 4)

            here = at["ssm_out"]
            with dve.Fori(0, 2) as i:
                for u in range(4):
                    m = 4 * i + u
                    dve.wait_ge(h_split, here.h + m + 1)
                    dve.tensor_tensor(h_low[:, m, :], za[:, m, :], h_high[:, m, :].bitcast(F32), sub).then_inc(h_ready, 1)
                    dve.wait_ge(h_ready, here.h + m + 1)
                    dve.wait_ge(slab_used, here.slab + 2 * i + u // 2 + 1)
                    dve.wait_ge(sg_loaded[u % 2], 16 * (2 * i + u // 2 + 1))
                    dve.tensor_tensor(mb[:, m, :], stage[u % 2][:, :], unit[u][:, :], mul).then_inc(unit_free[u], 1)
            here = at["conv_out"]
            with dve.Fori(0, KD // 2) as i:
                for e in range(2):
                    m = 2 * i + e
                    dve.wait_ge(slab_used, here.slab + m + 1)
                    dve.wait_ge(sg_loaded[e], 16 * (4 + i + 1))
                    dve.tensor_tensor(merged[:, :], stage[e][:, :], unit[e][:, :], mul).then_inc(unit_free[e], 1)
                    dve.wait_ge(unit_free[e], here.unit[e] + i + 1)
                    dve.tensor_tensor(merged[:, :], merged[:, :], mb[:, m, :], add).then_inc(merged_done, 1)
                    dve.wait_ge(g_split, here.g + m + 1)
                    dve.tensor_tensor(g_low[:, m, :], merged[:, :], g_high[:, m, :].bitcast(F32), sub).then_inc(g_ready, 1)
                    dve.wait_ge(g_ready, here.g + m + 1)
            dve.wait_ge(x_back, 16 * KD)
            own.then(dve.memset(s1[:, :], 0.0))
            down("w_out", mod[:, GT[1]:GT[1] + KD], 2)
            norm(2, at["norm2"].h, at["norm2"].unit[A_])
            for n in range(3):
                up("ffn2", n, False)
                down(f"ffn2.down{n}", gate[1][:, :])
            for m in range(0, KD, 2):
                dve.wait_ge(out_full, m + 1)
                dve.tensor_copy(o_rows[:, :, m * P:(m + 1) * P],
                                unit[A_][:, :].rearrange("p (j n) -> p j n", n=P)).then_inc(unit_free[A_], 1)
            dve.wait_ge(root_done, 4)
            own.then(dve.reciprocal(rms[:, :], rms[:, :]))
            dve.wait_ge(gf_loaded, 16)
            for j in range(J):
                dve.scalar_tensor_tensor(out=o_out[:, j, :], in0=o_rows[:, j, :], scalar=rms[:, j:j + 1],
                                         in1=gf_row[:, :], op0=mul, op1=mul).then_inc(o_final, 1)


_INS = ['x', 'c', 'w_ada', 'b_ada', 'g_ffn1', 'w1_a', 'w3_a', 'w2_a', 'g_mix', 'w_in', 'conv_w', 'w_conv_out',
        'a_re', 'a_im', 'b_re', 'b_im', 'c_re', 'c_im', 'log_dt', 'd_skip', 'w_glu', 'w_ssm_out', 'w_out',
        'g_ffn2', 'w1_b', 'w3_b', 'w2_b', 'g_final']


def kernel(**inputs):
    import numpy as _np
    import concourse.bacc as _bacc
    from concourse import mybir as _mybir
    from concourse.bass_utils import run_bass_kernel_spmd as _run

    nc = _bacc.Bacc("TRN2", target_bir_lowering=False, num_devices=1, dynamic_dma_scratch_size=1024)
    arrays, args = {}, {}
    for name in _INS:
        v = _np.ascontiguousarray(inputs[name])
        arrays[f"in_{name}"] = v
        args[name] = nc.dram_tensor(f"in_{name}", v.shape, _mybir.dt.from_np(v.dtype), kind="ExternalInput").ap()
    out = nc.dram_tensor("out", (1, T, D), _mybir.dt.float32, kind="ExternalOutput").ap()
    block_kernel(nc, args, out)
    r = _run(nc, [arrays], core_ids=[0])
    return r.results[0]["out"]
```

```python
from contextlib import ExitStack

import concourse.bass as bass
from concourse import mybir

F32 = mybir.dt.float32
F32R = mybir.dt.float32r
ACT = mybir.ActivationFunctionType
ALU = mybir.AluOpType

P = 128
D = 1024
T = 1024
KD = D // P
HALF = T // 2
J = 8
C = T // J
FF = 2816
FT = FF // P
CHUNKS = ((0, 8), (8, 8), (16, 6))
G, H, NS = 32, 16, 64
KP = G // 2
NT = G * H // P
LEVELS = 7
PAD = C // 2
NMOD = 9 * KD
EPS = 1e-6
PI = 3.141592653589793
ROUND = 12582912.0
TWO_PI = (6.28125, 0.0019350051879882812, 3.0199159819104966e-07)

A_, B_, C_, D_ = range(4)


def phases():
    out = [("setup", 0, (2, 1, 4, 4), 0, 2 * KD)]

    def ffn(name, ada):
        for n, (_, count) in enumerate(CHUNKS):
            c = count if ada and n < 2 else 0
            out.append((f"{name}.up{n}", 2 * count, (count, count, c, 0), count, 0))
            out.append((f"{name}.down{n}", KD, (0, 0, 4, 4), 0, 0))

    ffn("ffn1", True)
    out.append(("norm1", 0, (1, 0, 0, 0), 0, 2 * KD))
    out.append(("u", NT, (2, 2, 1, 0), 0, 0))
    out.append(("gates", 16, (8, 8, 8, 8), 0, 0))
    out.append(("conv_in0", 12, (4, 4, 4, 0), 0, 0))
    out.append(("glu", 4, (1, 1, 1, 1), 0, 0))
    out.append(("conv_in1", 12, (4, 4, 4, 0), 0, 0))
    out.append(("ssm_out", 4, (2, 2, 2, 2), 0, KD))
    out.append(("conv_out", KD, (4, 4, 0, 0), KD, 0))
    out.append(("w_out", KD, (0, 0, 4, 4), 0, 0))
    out.append(("norm2", 0, (1, 0, 0, 0), 0, 2 * KD))
    ffn("ffn2", False)
    out.append(("end", 0, (0, 0, 0, 0), 0, 0))
    return out


class At:

    def __init__(self, slab, unit, g, h):
        self.slab, self.unit, self.g, self.h = slab, unit, g, h


def starts():
    at, slab, unit, g, h = {}, 0, [0, 0, 0, 0], 0, 0
    for name, slabs, units, gs, hs in phases():
        at[name] = At(slab, tuple(unit), g, h)
        slab, g, h = slab + slabs, g + gs, h + hs
        unit = [a + b for a, b in zip(unit, units)]
    return at


def column(ap, m):
    return ap.rearrange("p (m o) -> p m o", o=1)[:, m, :]


class Steps:

    def __init__(self, engine, semaphore):
        self.engine, self.semaphore, self.base, self.k = engine, semaphore, 0, 0

    def then(self, instruction):
        instruction.then_inc(self.semaphore, 1)
        self.k += 1
        self.engine.wait_ge(self.semaphore, self.base + self.k)

    def enter(self, i, each):
        self.start = self.base + self.k
        self.base, self.k, self.each = self.start + i * each, 0, each

    def leave(self, turns):
        assert self.k == self.each, (self.k, self.each)
        self.base, self.k = self.start + turns * self.each, 0


def block_kernel(nc, a, out):
    at = starts()
    with ExitStack() as ctx:
        base = (nc.sbuf_base + 31) // 32 * 32
        top = [base]

        def region(nbytes):
            at_ = top[0]
            top[0] += nbytes
            return at_

        KB = 1024
        rX, rH, rM, rA = region(32 * KB), region(64 * KB), region(64 * KB), region(16 * KB)
        rRaw, rW, rS = region(16 * KB), region(16 * KB), region(8 * KB)

        def sb(name, shape, offset, dt=F32):
            return nc.alloc_sbuf_tensor_at(name, shape, dt, offset=offset)

        raw = sb("raw", [P, 4, KD, P], rRaw)
        w_high = sb("w_high", [P, 2, KD, P], rW, F32R)
        w_low = sb("w_low", [P, 2, KD, P], rW + 8 * KB, F32R)
        x_res = sb("x_res", [P, KD, T], rX)
        h_high = sb("h_high", [P, KD, T], rH, F32R)
        h_low = sb("h_low", [P, KD, T], rH + 32 * KB, F32R)
        g_high = sb("g_high", [P, KD, T], rM, F32R)
        g_low = sb("g_low", [P, KD, T], rM + 32 * KB, F32R)
        s0 = sb("s0", [P, T], rS)
        s1 = sb("s1", [P, T], rS + 4 * KB)
        stage = (s0, s1)
        x_rows = sb("x_rows", [P, J, D], rH)
        ada_first = sb("ada_first", [P, KD, 16 * P], rM)
        ada_first_sum = sb("ada_first_sum", [P, 16 * P], rH + 32 * KB)
        ada_raw = sb("ada_raw", [P, KD, 4 * P], rA)
        rstd = sb("rstd", [P, T], rA)
        xr = sb("xr", [P, 4, HALF], rA + 4 * KB)
        u_all = sb("u_all", [P, NT, T], rM)
        y_all = sb("y_all", [P, NT, T], rM + 16 * KB)
        s_high = sb("s_high", [P, NT, T], rM + 32 * KB, F32R)
        s_low = sb("s_low", [P, NT, T], rM + 48 * KB, F32R)
        y_chunk = sb("y_chunk", [P, 8, C], rM + 32 * KB)
        c_rows = sb("c_rows", [H, 2, KP, P], rM + 36 * KB)
        ca = sb("ca", [P, 4, 2, 9, H], rX)
        xt = sb("xt", [P, 4, 2, P], rX + 4608)
        toep = sb("toep", [P, 8, P], rX + 8704)
        sc_a = sb("sc_a", [P, 4, 2, PAD + C], rX + 12800)
        sc_b = sb("sc_b", [P, 4, 2, PAD + C], rX + 18944)
        u_chunk = sb("u_chunk", [P, 8, C], rX + 25088)
        ba = sb("ba", [P, 4, 2, J, H], rA)
        k_rows = sb("k_rows", [H, 8, P], rA + 4 * KB)
        b_now = sb("b_now", [P, 4, 2, H], rA + 8 * KB)
        za = sb("za", [P, KD, T], rX)
        gv = sb("gv", [P, J + 2, C], rA)
        taps = sb("taps", [P, T], rA + 5 * KB)
        mb = sb("mb", [P, KD, T], rX)
        merged = sb("merged", [P, T], rA)
        o_rows = sb("o_rows", [P, J, D], rH)
        o_out = sb("o_out", [P, J, D], rH + 32 * KB)
        gf_row = sb("gf_row", [P, D], rA)
        sumsq = sb("sumsq", [P, J], rA + 4 * KB)
        rms = sb("rms", [P, J], rA + 4 * KB + 64)

        def small(name, shape, dt=F32):
            size = 4
            for n in shape[1:]:
                size *= n
            return sb(name, shape, region((size + 31) // 32 * 32), dt)

        ident = small("ident", [P, P])
        ones = small("ones", [P, P])
        v_rows = small("v_rows", [P, P])
        d_rows = small("d_rows", [NT, P])
        vt = small("vt", [P, P + NT])
        cond = small("cond", [P, KD])
        mod = small("mod", [P, NMOD])
        scale = [small(f"scale{n}", [P, KD]) for n in range(3)]
        gate = [small(f"gate{n}", [P, KD]) for n in (0, 2)]
        eps = small("eps", [P, 1])
        ada_sum = small("ada_sum", [P, 4 * P])
        lam = sb("lam", [P, 2, KP], rM + 52 * KB)
        dt_ = sb("dt_", [P, KP], rM + 52 * KB + 128)
        q = [sb(f"q{n}", [P, KP], rM + 52 * KB + 192 + 64 * n) for n in range(8)]
        b_in = sb("b_in", [P, 2, KP, H], rM + 53 * KB)
        pv = sb("pv", [P, 2, J, KP], rM + 55 * KB)
        tmp = sb("tmp", [P, 2, 4 * 9 * H], rM + 59 * KB)
        pw = sb("pw", [P, 2, 9, KP], rA + 9 * KB)
        lv = sb("lv", [P, LEVELS, 3, KP], rA + 9 * KB + 1152)
        b_bar = sb("b_bar", [P, 2, KP, H], rA + 9 * KB + 2496)
        c_mat = sb("c_mat", [P, 2, KP, H], rA + 9 * KB + 4544)
        assert top[0] <= nc.sbuf_usable_end, top[0]
        B_ADA, GN, CW, DS = 8, (80, 88, 96), 104, P
        SH, SC, GT = (0, 24, 48), (8, 32, 56), (16, 40, 64)

        unit = [ctx.enter_context(nc.psum_tensor(f"unit_{x}", [P, T], F32)) for x in "abcd"]

        x_kept = nc.dram_tensor("x_kept", (P, KD * T), F32).ap()
        u_kept = nc.dram_tensor("u_kept", (NT, P, T), F32).ap()
        y_kept = nc.dram_tensor("y_kept", (NT, P, T), F32).ap()
        sg_kept = nc.dram_tensor("sg_kept", (16, P, T), F32).ap()

        def sem(name):
            return ctx.enter_context(nc.semaphore(name))

        slab_loaded = [sem(f"slab_loaded{r}") for r in range(4)]
        high_split = sem("high_split")
        slab_split = sem("slab_split")
        slab_used = sem("slab_used")
        unit_free = [sem(f"unit_free_{x}") for x in "abcd"]
        rows_loaded = sem("rows_loaded")
        x_loaded = [sem(f"x_loaded{j}") for j in range(J)]
        ada_loaded = [sem(f"ada_loaded{k}") for k in range(KD)]
        ada_more = sem("ada_more")
        ada_summed = sem("ada_summed")
        consts = sem("consts")
        setup_full = sem("setup_full")
        vt_ready = sem("vt_ready")
        cond_ready = sem("cond_ready")
        ada_full = sem("ada_full")
        x_final = sem("x_final")
        sq_done = sem("sq_done")
        acc_done = sem("acc_done")
        stat_full = sem("stat_full")
        root_done = sem("root_done")
        xr_done = sem("xr_done")
        h_split = sem("h_split")
        h_ready = sem("h_ready")
        g_split = sem("g_split")
        g_ready = sem("g_ready")
        x_kept_done = sem("x_kept_done")
        lam_loaded = sem("lam_loaded")
        b_loaded = sem("b_loaded")
        u_kept_done = sem("u_kept_done")
        trig = sem("trig")
        trig_act = sem("trig_act")
        ba_ready = sem("ba_ready")
        ssm_full = sem("ssm_full")
        u_loaded = sem("u_loaded")
        toep_loaded = sem("toep_loaded")
        toep_clear = sem("toep_clear")
        scan_step = sem("scan_step")
        scan_done = sem("scan_done")
        sg_saved = [sem("sg_saved0"), sem("sg_saved1")]
        sg_loaded = [sem("sg_loaded0"), sem("sg_loaded1")]
        y_saved = sem("y_saved")
        y_loaded = sem("y_loaded")
        s_sum = sem("s_sum")
        s_split = sem("s_split")
        s_ready = sem("s_ready")
        gated = sem("gated")
        merged_done = sem("merged_done")
        x_back = sem("x_back")
        gf_loaded = sem("gf_loaded")
        out_full = sem("out_full")
        o_final = sem("o_final")
        stored = sem("stored")
        act_step = sem("act_step")
        dve_step = sem("dve_step")

        block = ctx.enter_context(nc.Block())

        @block.sync
        def _(sp):
            def row(dst, src, first):
                n = src.shape[0]
                sp.dma_start(dst[first:first + n, :], src).then_inc(rows_loaded, 16)

            def tiles(ap):
                return ap.rearrange("(m p) -> m p", p=P)

            row(v_rows, tiles(a["c"][0]), 0)
            row(v_rows, tiles(a["b_ada"][0]), B_ADA)
            for n, name in enumerate(("g_ffn1", "g_mix", "g_ffn2")):
                row(v_rows, tiles(a[name][0]), GN[n])
            row(v_rows, a["conv_w"][0].rearrange("k (m p) -> (k m) p", p=P), CW)
            row(d_rows, tiles(a["d_skip"][0]), 0)
            x_tok = a["x"][0].rearrange("(c j) n -> c j n", j=J)
            for j in range(J):
                sp.dma_start(x_rows[:, j, :], x_tok[:, j, :]).then_inc(x_loaded[j], 16)
            ada = a["w_ada"][0].rearrange("(k p) n -> p k n", p=P)
            for k in range(KD):
                if k == KD - 2:
                    for r, w in enumerate((a["w1_a"][0], a["w3_a"][0])):
                        sp.dma_start(raw[:, r, :, :], w.rearrange("(k p) (f n) -> p k f n", p=P, n=P)[:, :, 0, :]).then_inc(
                            slab_loaded[r], 16)
                sp.dma_start(ada_first[:, k, :], ada[:, k, 0:16 * P]).then_inc(ada_loaded[k], 16)

            def load(s, r, src, tiles_k=KD):
                if not (isinstance(s, int) and s < 4):
                    sp.wait_ge(slab_split, s - 3)
                sp.dma_start(raw[:, r, 0:tiles_k, :], src).then_inc(slab_loaded[r], 16)

            def ffn(name, w1, w3, w2, with_ada):
                v1 = w1.rearrange("(k p) (f n) -> p k f n", p=P, n=P)
                v3 = w3.rearrange("(k p) (f n) -> p k f n", p=P, n=P)
                v2 = w2.rearrange("(k p) (m n) -> p k m n", p=P, n=P)
                for n, (f0, count) in enumerate(CHUNKS):
                    here = at[f"{name}.up{n}"].slab
                    many = (4, 3, 0)[n] if with_ada else 0

                    def up(i, e0=0):
                        for e in range(e0, 2):
                            load(here + 4 * i + 2 * e, 2 * e, v1[:, :, f0 + 2 * i + e, :])
                            load(here + 4 * i + 2 * e + 1, 2 * e + 1, v3[:, :, f0 + 2 * i + e, :])
                        if many:
                            first, turn0 = ((16, 0), (48, 8))[n]
                            cols = ada[:, :, first * P:(first + many * count) * P].rearrange(
                                "p k (i m) -> p k i m", m=many * P)
                            if n == 0:
                                sp.wait_ge(h_ready, 2 * KD)
                            for e in range(2):
                                sp.wait_ge(ada_summed, turn0 + 1 + 2 * i + e)
                                sp.dma_start(ada_raw[:, :, 0:many * P], cols[:, :, 2 * i + e, :]).then_inc(ada_more, 16)

                    up(0, 1 if with_ada and n == 0 else 0)
                    with sp.Fori(1, count // 2) as i:
                        up(i)
                    here2 = at[f"{name}.down{n}"].slab
                    with sp.Fori(0, KD // 4) as i:
                        for r in range(4):
                            load(here2 + 4 * i + r, r, v2[:, f0:f0 + count, 4 * i + r, :], count)

            ffn("ffn1", a["w1_a"][0], a["w3_a"][0], a["w2_a"][0], True)

            w_in = a["w_in"][0].rearrange("(k p) (m n) -> p k m n", p=P, n=P)
            for r in range(NT):
                load(at["u"].slab + r, r, w_in[:, :, 24 + r, :])
            for first, where in ((36, 0), (28, 8)):
                with sp.Fori(0, 2) as i:
                    for r in range(4):
                        load(at["gates"].slab + where + 4 * i + r, r, w_in[:, :, first + 4 * i + r, :])

            def conv_in(name, m0):
                n = 0
                for m in range(m0, m0 + 4):
                    for col in (8, 16, 0):
                        load(at[name].slab + n, n % 4, w_in[:, :, col + m, :])
                        n += 1

            conv_in("conv_in0", 0)
            glu = a["w_glu"][0].rearrange("(k p) (m n) -> p k m n", p=P, n=P)
            for r in range(NT):
                load(at["glu"].slab + r, r, glu[:, :, r, :], NT)
            conv_in("conv_in1", 4)
            w_so = a["w_ssm_out"][0].rearrange("(k p) (m n) -> p k m n", p=P, n=2 * P)
            for r in range(4):
                sp.wait_ge(slab_split, at["ssm_out"].slab + r - 3)
                sp.dma_start(raw[:, r, :, :].rearrange("p (k e) n -> p k (e n)", e=2),
                             w_so[:, :, r, :]).then_inc(slab_loaded[r], 16)
            for name, w in (("conv_out", a["w_conv_out"][0]), ("w_out", a["w_out"][0])):
                v = w.rearrange("(k p) (m n) -> p k m n", p=P, n=P)
                with sp.Fori(0, 2) as i:
                    for r in range(4):
                        load(at[name].slab + 4 * i + r, r, v[:, :, 4 * i + r, :])
            ffn("ffn2", a["w1_b"][0], a["w3_b"][0], a["w2_b"][0], False)
            out_tok = out[0].rearrange("(c j) n -> c j n", j=J)
            for j in range(J):
                sp.wait_ge(o_final, j + 1)
                sp.dma_start(out_tok[:, j, :], o_out[:, j, :]).then_inc(stored, 16)
            sp.wait_ge(stored, 16 * J)

        @block.gpsimd
        def _(pool):
            pool.memset(ident[:, :], 0.0).then_inc(consts, 1)
            pool.memset(ones[:, :], 1.0).then_inc(consts, 1)
            pool.memset(eps[:, :], EPS).then_inc(consts, 1)
            pool.wait_ge(consts, 3)
            pool.affine_select(out=ident[:, :], in_=ident[:, :], compare_op=ALU.not_equal, fill=1.0,
                               base=0, pattern=[[-1, P]], channel_multiplier=1).then_inc(consts, 1)

            one = ones[:, :].rearrange("p (o n) -> p o n", o=1).to_broadcast([P, KD, P])

            def split(i, first):
                for r in range(4):
                    pool.wait_ge(slab_loaded[r], 16 * (i + 1))
                    if not first or r >= 2:
                        pool.wait_ge(slab_used, 4 * i + r - 1)
                    high = w_high[:, r % 2, :, :]
                    pool.tensor_tensor(high, raw[:, r, :, :], one, ALU.mult).then_inc(high_split, 1)
                    pool.wait_ge(high_split, 4 * i + r + 1)
                    pool.tensor_tensor(w_low[:, r % 2, :, :], raw[:, r, :, :], high.bitcast(F32),
                                       ALU.subtract).then_inc(slab_split, 1)

            split(0, True)
            with pool.Fori(1, at["end"].slab // 4) as i:
                split(i, False)

        @block.tensor
        def _(pe):
            def take(u, uses):
                if not (isinstance(uses, int) and uses == 0):
                    pe.wait_ge(unit_free[u], uses)

            def product(u, slot, high, low, kts, cols=slice(0, P), ready=None, row=None):
                for k in range(kts):
                    if ready is not None:
                        pe.wait_ge(ready[0], ready[1] + k + 1)
                    wk = k if row is None else row(k)
                    wh = w_high[:, slot, wk, cols]
                    wl = w_low[:, slot, wk, cols]
                    for part, (w, x) in enumerate(((wh, high), (wh, low), (wl, high))):
                        for half in range(2):
                            t = slice(512 * half, 512 * half + 512)
                            last = pe.matmul(unit[u][:, t], w, x[:, k, t], start=(k == 0 and part == 0),
                                             stop=(k == kts - 1 and part == 2))
                return last

            def slab(s, slot, u, uses, high, low, kts, ready=None):
                pe.wait_ge(slab_split, s + 1)
                take(u, uses)
                product(u, slot, high, low, kts, ready=ready).then_inc(slab_used, 1)

            pe.wait_ge(consts, 4)
            pe.wait_ge(rows_loaded, 7 * 16)
            pe.transpose(unit[A_][:, 0:P], v_rows[:, :], ident[:, :])
            pe.transpose(unit[A_][:, P:P + NT], d_rows[:, :], ident[0:NT, 0:NT]).then_inc(setup_full, 1)
            for j in range(J):
                pe.wait_ge(x_loaded[j], 16)
                u, uses = (C_, D_)[j % 2], j // 2
                take(u, uses)
                for m in range(KD):
                    last = pe.transpose(unit[u][:, m * P:(m + 1) * P], x_rows[:, j, m * P:(m + 1) * P], ident[:, :])
                last.then_inc(setup_full, 1)

            def ada_tiles(w, count, u):
                for t in range(count):
                    last = pe.matmul(unit[u][:, t:t + 1], w[:, t * P:(t + 1) * P], ones[:, 0:1], start=True, stop=True)
                last.then_inc(ada_full, 1)

            def statistics(uses, added):
                take(A_, uses)
                for half in range(2):
                    t = slice(HALF * half, HALF * half + HALF)
                    pe.wait_ge(acc_done, added[half])
                    pe.matmul(unit[A_][:, t], ones[:, :], s1[:, t], start=True, stop=True).then_inc(stat_full, 1)

            statistics(1, (KD, 2 * KD))
            pe.wait_ge(ada_summed, 1)
            ada_tiles(ada_first_sum, 16, B_)

            def first_pair(s, uses, h0):
                pe.wait_ge(slab_split, s + 2)
                for u in (A_, B_):
                    take(u, uses[u])
                for half in range(2):
                    t = slice(HALF * half, HALF * half + HALF)
                    for k in range(KD):
                        pe.wait_ge(h_ready, h0 + KD * half + k + 1)
                        for u in (A_, B_):
                            wh, wl = w_high[:, u, k, :], w_low[:, u, k, :]
                            for part, (w, x) in enumerate(((wh, h_high), (wh, h_low), (wl, h_high))):
                                last = pe.matmul(unit[u][:, t], w, x[:, k, t], start=(k == 0 and part == 0),
                                                 stop=(k == KD - 1 and part == 2))
                            if half == 1 and k == KD - 1:
                                last.then_inc(slab_used, 1)

            def up(name, n, i, with_ada):
                here = at[f"{name}.up{n}"]
                if isinstance(i, int):
                    first_pair(here.slab, here.unit, here.h - 2 * KD)
                else:
                    slab(here.slab + 2 * i, 0, A_, here.unit[A_] + i, h_high, h_low, KD)
                    slab(here.slab + 2 * i + 1, 1, B_, here.unit[B_] + i, h_high, h_low, KD)
                if with_ada and n < 2:
                    pe.wait_ge(ada_summed, 8 * n + i + 2)
                    take(C_, here.unit[C_] + i)
                    ada_tiles(ada_sum, 4 - n, C_)

            def down(name, kts, i):
                here = at[name]
                for e in range(2):
                    slab(here.slab + 2 * i + e, e, C_ + e, here.unit[C_ + e] + i, g_high, g_low, kts,
                         (g_ready, here.g - kts))

            def ffn(name, with_ada):
                for n, (_, count) in enumerate(CHUNKS):
                    if n == 0:
                        up(name, 0, 0, with_ada)
                    with pe.Fori(1 if n == 0 else 0, count) as i:
                        up(name, n, i, with_ada)
                    with pe.Fori(0, KD // 2) as i:
                        down(f"{name}.down{n}", count, i)

            ffn("ffn1", True)
            statistics(at["norm1"].unit[A_], (4 * KD - 1, 4 * KD))

            here = at["u"]
            first_pair(here.slab, here.unit, here.h - 2 * KD)
            for t in range(2, NT):
                slab(here.slab + t, t % 2, t % 2, here.unit[t % 2] + t // 2, h_high, h_low, KD)
            pe.wait_ge(b_loaded, 16 * 4)
            take(C_, here.unit[C_])
            for part in range(2):
                for k in range(KP):
                    col = (part * KP + k) * H
                    last = pe.transpose(unit[C_][:, col:col + H], c_rows[:, part, k, :], ident[0:H, 0:H])
            last.then_inc(ssm_full, 1)

            here = at["gates"]

            def gates(t):
                def gate_slab(q_):
                    slab(here.slab + 4 * t + q_, q_ % 2, q_ % 2, here.unit[q_ % 2] + 2 * t + q_ // 2, h_high, h_low, KD)

                pe.wait_ge(ba_ready, t + 1)
                take(D_, here.unit[D_] + 2 * t)
                take(C_, here.unit[C_] + 2 * t)
                for kk in range(4):
                    for part in range(2):
                        col = (2 * kk + part) * P
                        last = pe.transpose(unit[C_][:, col:col + P],
                                            ba[:, kk, part, :, :].rearrange("p j h -> p (j h)"), ident[:, :])
                last.then_inc(ssm_full, 1)
                for g2 in range(2):
                    rows = slice(NS * g2, NS * g2 + NS)
                    for kk in range(4):
                        col = (4 * g2 + kk) * P
                        for part in range(2):
                            last = pe.matmul(unit[D_][0:H, col:col + P], b_now[rows, kk, part, :],
                                             ca[rows, kk, part, 0:8, :].rearrange("p d h -> p (d h)"),
                                             start=(part == 0), stop=(part == 1))
                last.then_inc(ssm_full, 1)
                pe.wait_ge(unit_free[C_], here.unit[C_] + 2 * t + 1)
                pe.wait_ge(u_loaded, 128 * (t + 1))
                for g2 in range(2):
                    for kk in range(4):
                        for part in range(2):
                            col = (2 * kk + part) * P
                            last = pe.matmul(unit[C_][NS * g2:NS * g2 + NS, col:col + P],
                                             xt[:, kk, part, NS * g2:NS * g2 + NS], u_chunk[:, 2 * kk + g2, :],
                                             start=True, stop=True)
                last.then_inc(ssm_full, 1)
                gate_slab(0)
                gate_slab(1)
                gate_slab(2)
                pe.wait_ge(scan_done, t + 1)
                pe.wait_ge(toep_loaded, 128 * (t + 1))
                take(D_, here.unit[D_] + 2 * t + 1)
                for g2 in range(2):
                    rows = slice(NS * g2, NS * g2 + NS)
                    for kk in range(4):
                        dst = unit[D_][:, (4 * g2 + kk) * P:(4 * g2 + kk + 1) * P]
                        pe.matmul(dst, toep[:, 4 * g2 + kk, :], u_chunk[:, 2 * kk + g2, :], start=True, stop=False)
                        for part in range(2):
                            last = pe.matmul(dst, ca[rows, kk, part, 1:9, :].rearrange("p d h -> p (d h)"),
                                             sc_b[rows, kk, part, PAD:], start=False, stop=(part == 1))
                last.then_inc(ssm_full, 1)
                gate_slab(3)

            with pe.Fori(0, NT) as t:
                gates(t)

            def conv_in(name):
                here = at[name]
                with pe.Fori(0, 2) as i:
                    for e in range(2):
                        for n, u in enumerate((A_, B_, C_)):
                            slab(here.slab + 6 * i + 3 * e + n, (3 * e + n) % 2, u, here.unit[u] + 2 * i + e,
                                 h_high, h_low, KD)

            conv_in("conv_in0")
            here = at["glu"]
            for t in range(NT):
                slab(here.slab + t, t % 2, t, here.unit[t], s_high, s_low, NT, (s_ready, 0))
            conv_in("conv_in1")
            here = at["ssm_out"]
            with pe.Fori(0, 2) as i:
                for e in range(2):
                    pe.wait_ge(slab_split, here.slab + 2 * i + e + 1)
                    for half in range(2):
                        u = 2 * e + half
                        take(u, here.unit[u] + i)
                        last = product(u, e, s_high, s_low, NT, ready=(s_ready, NT), row=lambda k: 2 * k + half)
                    last.then_inc(slab_used, 1)
            here = at["conv_out"]
            with pe.Fori(0, KD // 2) as i:
                for e in range(2):
                    slab(here.slab + 2 * i + e, e, e, here.unit[e] + i, h_high, h_low, KD, (h_ready, here.h - KD))
            with pe.Fori(0, KD // 2) as i:
                down("w_out", KD, i)
            statistics(at["norm2"].unit[A_], (6 * KD - 1, 6 * KD))
            ffn("ffn2", False)

            last_down = at["ffn2.down2"]
            ends = at["end"]
            for m in range(KD):
                pe.wait_ge(unit_free[C_ + m % 2], last_down.unit[C_ + m % 2] + m // 2 + 1)
                take(m % 2, ends.unit[m % 2] + m // 2)
                for j in range(J):
                    last = pe.transpose(unit[m % 2][:, j * P:(j + 1) * P], x_res[:, m, j * P:(j + 1) * P], ident[:, :])
                last.then_inc(out_full, 1)

        @block.scalar
        def _(act):
            own = Steps(act, act_step)

            act.wait_ge(vt_ready, 1)
            act.activation(cond[:, :], vt[:, 0:KD], ACT.Silu).then_inc(cond_ready, 1)

            def square(m, half, added):
                t = slice(HALF * half, HALF * half + HALF)
                if added is not None:
                    act.wait_ge(acc_done, added)
                act.activation(s0[:, t], x_res[:, m, t], ACT.Square).then_inc(sq_done, 1)

            for half in range(2):
                for j in (4 * half + 1, 4 * half + 3):
                    act.wait_ge(setup_full, 2 + j)
                    act.activation(x_res[:, :, j * C:(j + 1) * C], unit[D_][:, :].rearrange("p (m c) -> p m c", c=C),
                                   ACT.Copy).then_inc(unit_free[D_], 1)
                act.wait_ge(unit_free[C_], 2 * half + 2)
                act.wait_ge(unit_free[D_], 2 * half + 2)
                square(0, half, KD * half if half else None)
                with act.Fori(1, KD) as m:
                    square(m, half, KD * half + m)

            def norm(n, h0):
                for half in range(2):
                    t = slice(HALF * half, HALF * half + HALF)
                    act.wait_ge(stat_full, 2 * n + half + 1)
                    act.activation(s0[:, t], unit[A_][:, t], ACT.Sqrt, bias=eps[:, 0:1],
                                   scale=1.0 / D).then_inc(root_done, 1)
                if n == 1:
                    act.dma_start(x_kept, x_res[:, :, :].rearrange("p k t -> p (k t)")).then_inc(x_kept_done, 16)
                for step in range(2 * KD):
                    half, m = divmod(step, KD)
                    t = slice(HALF * half, HALF * half + HALF)
                    tile = xr[:, step % 4, :]
                    act.wait_ge(xr_done, 2 * KD * n + step + 1)
                    own.then(act.activation(tile, tile, ACT.Identity, scale=scale[n][:, m:m + 1],
                                            bias=mod[:, SH[n] + m:SH[n] + m + 1]))
                    act.activation(h_high[:, m, t], tile, ACT.Copy).then_inc(h_split, 1)

            norm(0, 0)

            def up(name, n):
                here = at[f"{name}.up{n}"]
                with act.Fori(0, CHUNKS[n][1]) as i:
                    act.wait_ge(slab_used, here.slab + 2 * i + 1)
                    act.activation(s0[:, :], unit[A_][:, :], ACT.Silu).then_inc(unit_free[A_], 1)
                    act.wait_ge(unit_free[B_], here.unit[B_] + i + 1)
                    act.activation(g_high[:, i, :], s1[:, :], ACT.Copy).then_inc(g_split, 1)

            def down_squares(n):
                with act.Fori(0, KD) as m:
                    for half in range(2):
                        act.wait_ge(x_final, 2 * KD * (n - 1) + 2 * m + half + 1)
                        square(m, half, 2 * KD * n + 2 * m + half - 1)

            for n in range(3):
                up("ffn1", n)
            down_squares(1)
            norm(1, at["norm1"].h)

            def as_states(ap):
                return ap.rearrange("(k g) p -> (g p) k", g=2)

            with nc.allow_non_contiguous_dma(reason="small parameter tables"):
                act.dma_start(lam[:, 0, :], as_states(a["a_re"][0])).then_inc(lam_loaded, 16)
                act.dma_start(lam[:, 1, :], as_states(a["a_im"][0])).then_inc(lam_loaded, 16)
                for g2 in range(2):
                    per = a["log_dt"][0].rearrange("(k g) -> g k", g=2)[g2:g2 + 1, :]
                    act.dma_start(dt_[NS * g2:NS * g2 + NS, :], per.to_broadcast([NS, KP])).then_inc(lam_loaded, 16)
                for part, (b, c) in enumerate((("b_re", "c_re"), ("b_im", "c_im"))):
                    act.dma_start(b_in[:, part, :, :], a[b][0].rearrange("(k g) p h -> (g p) k h", g=2)).then_inc(b_loaded, 16)
                    act.dma_start(c_rows[:, part, :, :].rearrange("h k (g p) -> h (k g) p", g=2),
                                  a[c][0].rearrange("g h p -> h g p")).then_inc(b_loaded, 16)
            act.wait_ge(lam_loaded, 64)
            act.activation(dt_[:, :], dt_[:, :], ACT.Exp).then_inc(trig_act, 1)
            act.wait_ge(trig, 1)
            act.activation(q[3][:, :], q[0][:, :], ACT.Exp).then_inc(trig_act, 1)
            act.wait_ge(trig, 2)
            act.activation(q[4][:, :], q[1][:, :], ACT.Sin).then_inc(trig_act, 1)
            act.activation(q[5][:, :], q[2][:, :], ACT.Sin).then_inc(trig_act, 1)

            here = at["u"]
            for t in range(NT):
                act.wait_ge(slab_used, here.slab + t + 1)
                act.activation(u_all[:, t, :], unit[t % 2][:, :], ACT.Copy).then_inc(unit_free[t % 2], 1)
                act.wait_ge(unit_free[t % 2], here.unit[t % 2] + t // 2 + 1)
                act.dma_start(u_kept[t], u_all[:, t, :]).then_inc(u_kept_done, 16)
            act.wait_ge(u_kept_done, 16 * NT)

            here = at["gates"]

            def load_u(t):
                act.wait_ge(ssm_full, 1 + 4 * t)
                u_src = u_kept.rearrange("t (g h) (j c) -> j t h g c", h=H, j=J)
                for j in range(J):
                    act.dma_start(u_chunk[H * j:H * j + H, :, :], u_src[j][t]).then_inc(u_loaded, 16)

            def gates(t, first=False, last=False):
                def gate_slab(q_):
                    act.wait_ge(slab_used, here.slab + 4 * t + q_ + 1)
                    if not first or q_ >= 2:
                        act.wait_ge(sg_saved[q_ % 2], 16 * (2 * t + q_ // 2))
                    act.activation(stage[q_ % 2][:, :], unit[q_ % 2][:, :], ACT.Sigmoid).then_inc(unit_free[q_ % 2], 1)
                    act.wait_ge(unit_free[q_ % 2], here.unit[q_ % 2] + 2 * t + q_ // 2 + 1)
                    act.dma_start(sg_kept.rearrange("(t q) p n -> q t p n", q=4)[q_][t], stage[q_ % 2][:, :]).then_inc(sg_saved[q_ % 2], 16)

                act.wait_ge(ssm_full, 2 + 4 * t)
                act.activation(xt[:, :, :, :].rearrange("p a b n -> p (a b n)"), unit[C_][:, :], ACT.Copy).then_inc(unit_free[C_], 1)
                act.wait_ge(ssm_full, 3 + 4 * t)
                act.activation(k_rows[:, :, :].rearrange("h g n -> h (g n)"), unit[D_][0:H, :], ACT.Copy).then_inc(unit_free[D_], 1)
                act.wait_ge(unit_free[D_], here.unit[D_] + 2 * t + 1)
                if first:
                    act.wait_ge(toep_clear, 1)
                for j in range(J):
                    act.dma_start(toep[H * j:H * j + H, :, H * j:P], k_rows[:, :, 0:P - H * j]).then_inc(toep_loaded, 16)
                gate_slab(0)
                gate_slab(1)
                gate_slab(2)
                act.wait_ge(ssm_full, 5 + 4 * t)
                act.activation(y_chunk[:, :, :].rearrange("p g c -> p (g c)"), unit[D_][:, :], ACT.Copy).then_inc(unit_free[D_], 1)
                act.wait_ge(unit_free[D_], here.unit[D_] + 2 * t + 2)
                y_dst = y_kept.rearrange("t (k g h) (i c) -> i g t h k c", g=2, h=H, i=J)
                for i in range(J):
                    for g2 in range(2):
                        act.dma_start(y_dst[i][g2][t], y_chunk[H * i:H * i + H, 4 * g2:4 * g2 + 4, :]).then_inc(y_saved, 16)
                if not last:
                    load_u(t + 1)
                gate_slab(3)
                act.wait_ge(y_saved, 256 * (t + 1))
                act.dma_start(y_all[:, t, :], y_kept[t]).then_inc(y_loaded, 16)

            load_u(0)
            gates(0, first=True)
            with act.Fori(1, NT - 1) as t:
                gates(t)
            gates(NT - 1, last=True)

            for t in range(NT):
                act.wait_ge(s_sum, t + 1)
                own.then(act.activation(u_all[:, t, :], u_all[:, t, :], ACT.Gelu_apprx_tanh))
                act.activation(s_high[:, t, :], u_all[:, t, :], ACT.Copy).then_inc(s_split, 1)

            def conv_in(name):
                here = at[name]
                with act.Fori(0, 4) as m:
                    act.wait_ge(slab_used, here.slab + 3 * m + 1)
                    act.wait_ge(unit_free[B_], here.unit[B_] + m)
                    act.activation(s0[:, :], unit[A_][:, :], ACT.Copy).then_inc(unit_free[A_], 1)

            for stage_ in range(2):
                act.wait_ge(sg_saved[stage_], 16 * 8)
            conv_in("conv_in0")
            here = at["glu"]
            for t in range(NT):
                act.wait_ge(slab_used, here.slab + t + 1)
                if t >= 2:
                    act.wait_ge(gated, t - 1)
                else:
                    act.wait_ge(unit_free[B_], here.unit[B_])
                act.activation(stage[t % 2][:, :], unit[t][:, :], ACT.Sigmoid).then_inc(unit_free[t], 1)
            for t in range(NT):
                act.wait_ge(gated, t + 1)
                act.activation(s_high[:, t, :], u_all[:, t, :], ACT.Copy).then_inc(s_split, 1)
            conv_in("conv_in1")

            def sg_load(n, e):
                act.dma_start(stage[e][:, :], sg_kept[n]).then_inc(sg_loaded[e], 16)

            here = at["ssm_out"]
            act.wait_ge(unit_free[B_], here.unit[B_])
            act.wait_ge(unit_free[C_], here.unit[C_])
            sg_load(0, 0)
            sg_load(1, 1)
            act.wait_ge(slab_used, here.slab)
            with act.Fori(0, 2) as i:
                for u in range(4):
                    m = 4 * i + u
                    act.activation(h_high[:, m, :], za[:, m, :], ACT.Copy).then_inc(h_split, 1)
                    act.wait_ge(unit_free[u], here.unit[u] + i + 1)
                    sg_load(m + 2, u % 2)
            here = at["conv_out"]
            x_tiles = x_kept.rearrange("p (k t) -> k p t", k=KD)
            with nc.allow_non_contiguous_dma(reason="rows of 4 KiB"):
                def conv_out(i, more):
                    for e in range(2):
                        m = 2 * i + e
                        act.wait_ge(unit_free[e], here.unit[e] + i + 1)
                        if more:
                            sg_load(m + 10, e)
                        act.wait_ge(merged_done, m + 1)
                        act.activation(g_high[:, m, :], merged[:, :], ACT.Copy).then_inc(g_split, 1)
                        act.dma_start(x_res[:, m, :], x_tiles[m]).then_inc(x_back, 16)

                with act.Fori(0, KD // 2 - 1) as i:
                    conv_out(i, True)
                conv_out(KD // 2 - 1, False)
            down_squares(2)
            norm(2, at["norm2"].h)
            for n in range(3):
                up("ffn2", n)
            act.dma_start(gf_row[:, :], a["g_final"].rearrange("(o n) -> o n", o=1).to_broadcast([P, D])).then_inc(gf_loaded, 16)
            ends = at["end"]
            for m in range(1, KD, 2):
                act.wait_ge(out_full, m + 1)
                act.activation(o_rows[:, :, m * P:(m + 1) * P], unit[B_][:, :].rearrange("p (j n) -> p j n", n=P),
                               ACT.Copy).then_inc(unit_free[B_], 1)
            act.wait_ge(unit_free[A_], ends.unit[A_] + 4)
            act.wait_ge(unit_free[B_], ends.unit[B_] + 4)
            for j in range(J):
                own.then(act.activation(o_out[:, j, :], o_rows[:, j, :], ACT.Square, accum_out=sumsq[:, j:j + 1]))
            act.activation(rms[:, :], sumsq[:, :], ACT.Sqrt, bias=eps[:, 0:1], scale=1.0 / D).then_inc(root_done, 1)

        @block.vector
        def _(dve):
            own = Steps(dve, dve_step)
            mul, add, sub = ALU.mult, ALU.add, ALU.subtract

            dve.wait_ge(setup_full, 1)
            dve.tensor_copy(vt[:, :], unit[A_][:, 0:P + NT]).then_inc(vt_ready, 1)
            dve.wait_ge(vt_ready, 1)
            dve.sem_inc(unit_free[A_], 1)

            def accumulate(m, half, count):
                t = slice(HALF * half, HALF * half + HALF)
                dve.wait_ge(sq_done, count + 1)
                dve.tensor_tensor(s1[:, t], s1[:, t], s0[:, t], add).then_inc(acc_done, 1)
                dve.wait_ge(acc_done, count + 1)

            own.then(dve.memset(s1[:, :], 0.0))
            for half in range(2):
                for j in (4 * half, 4 * half + 2):
                    dve.wait_ge(setup_full, 2 + j)
                    dve.tensor_copy(x_res[:, :, j * C:(j + 1) * C],
                                    unit[C_][:, :].rearrange("p (m c) -> p m c", c=C)).then_inc(unit_free[C_], 1)
                with dve.Fori(0, KD) as m:
                    accumulate(m, half, KD * half + m)

            def ada_columns(dst, src, count, loaded=None):
                for k in range(KD):
                    if loaded is not None:
                        dve.wait_ge(loaded[k], 16)
                    by = cond[:, k:k + 1]
                    if k == 0:
                        last = dve.tensor_scalar(dst[:, 0:count], src[:, k, 0:count], by, None, mul)
                    else:
                        last = dve.scalar_tensor_tensor(out=dst[:, 0:count], in0=src[:, k, 0:count], scalar=by,
                                                        in1=dst[:, 0:count], op0=mul, op1=add)
                    if k < KD - 1:
                        own.then(last)
                last.then_inc(ada_summed, 1)

            def root(n, half):
                t = slice(HALF * half, HALF * half + HALF)
                dve.wait_ge(root_done, 2 * n + half + 1)
                own.then(dve.reciprocal(rstd[:, t], s0[:, t]))

            dve.wait_ge(cond_ready, 1)
            ada_columns(ada_first_sum, ada_first, 16 * P, ada_loaded)
            root(0, 0)
            root(0, 1)
            dve.sem_inc(unit_free[A_], 1)
            dve.wait_ge(ada_full, 1)
            dve.tensor_tensor(mod[:, 0:16], unit[B_][:, 0:16], vt[:, B_ADA:B_ADA + 16], add).then_inc(unit_free[B_], 1)
            dve.wait_ge(unit_free[B_], 1)

            def derive_scale(n):
                return dve.scalar_tensor_tensor(out=scale[n][:, :], in0=mod[:, SC[n]:SC[n] + KD], scalar=1.0,
                                                in1=vt[:, GN[n]:GN[n] + KD], op0=add, op1=mul)

            own.then(derive_scale(0))

            def norm(n, h0):
                def scaled(step):
                    half, m = divmod(step, KD)
                    t = slice(HALF * half, HALF * half + HALF)
                    if step >= 4:
                        dve.wait_ge(h_ready, h0 + step - 3)
                    dve.tensor_tensor(xr[:, step % 4, :], x_res[:, m, t], rstd[:, t], mul).then_inc(xr_done, 1)

                def low(step):
                    half, m = divmod(step, KD)
                    t = slice(HALF * half, HALF * half + HALF)
                    dve.wait_ge(h_split, h0 + step + 1)
                    dve.tensor_tensor(h_low[:, m, t], xr[:, step % 4, :], h_high[:, m, t].bitcast(F32),
                                      sub).then_inc(h_ready, 1)

                if n > 0:
                    root(n, 0)
                    dve.wait_ge(root_done, 2 * n + 2)
                    dve.sem_inc(unit_free[A_], 1)
                ahead = 3
                for step in range(ahead):
                    scaled(step)
                for step in range(2 * KD):
                    low(step)
                    if step + ahead == KD and n > 0:
                        root(n, 1)
                    if step + ahead < 2 * KD:
                        scaled(step + ahead)
                dve.wait_ge(h_ready, h0 + 2 * KD)

            norm(0, 0)

            def up(name, n, with_ada):
                here = at[f"{name}.up{n}"]
                with_ada = with_ada and n < 2
                with dve.Fori(0, CHUNKS[n][1]) as i:
                    if with_ada:
                        first, many = ((16, 4), (48, 3))[n]
                        own.enter(i, KD - 1)
                        dve.wait_ge(ada_more, 16 * (8 * n + i + 1))
                        ada_columns(ada_sum, ada_raw, many * P)
                    dve.wait_ge(unit_free[A_], here.unit[A_] + i + 1)
                    dve.wait_ge(slab_used, here.slab + 2 * i + 2)
                    dve.tensor_tensor(s1[:, :], s0[:, :], unit[B_][:, :], mul).then_inc(unit_free[B_], 1)
                    dve.wait_ge(g_split, here.g + i + 1)
                    dve.tensor_tensor(g_low[:, i, :], s1[:, :], g_high[:, i, :].bitcast(F32), sub).then_inc(g_ready, 1)
                    dve.wait_ge(g_ready, here.g + i + 1)
                    if with_ada:
                        cols = slice(first, first + 8 * many)
                        dve.wait_ge(ada_full, 8 * n + i + 2)
                        dve.tensor_tensor(
                            mod[:, cols].rearrange("p (i t) -> p i t", t=many)[:, i, :], unit[C_][:, 0:many],
                            vt[:, B_ADA + first:B_ADA + first + 8 * many].rearrange("p (i t) -> p i t", t=many)[:, i, :],
                            add).then_inc(unit_free[C_], 1)
                if with_ada:
                    own.leave(CHUNKS[n][1])

            def down(name, g, squares=None):
                here = at[name]
                with dve.Fori(0, KD // 2) as i:
                    for e in range(2):
                        m = 2 * i + e
                        dve.wait_ge(slab_used, here.slab + m + 1)
                        if squares is None:
                            dve.scalar_tensor_tensor(out=x_res[:, m, :], in0=unit[C_ + e][:, :], scalar=column(g, m),
                                                     in1=x_res[:, m, :], op0=mul, op1=add).then_inc(unit_free[C_ + e], 1)
                            continue
                        for half in range(2):
                            t = slice(HALF * half, HALF * half + HALF)
                            dve.scalar_tensor_tensor(out=x_res[:, m, t], in0=unit[C_ + e][:, t], scalar=column(g, m),
                                                     in1=x_res[:, m, t], op0=mul, op1=add).then_inc(x_final, 1)
                        for half in range(2):
                            accumulate(m, half, 2 * KD * squares + 2 * m + half)
                        dve.sem_inc(unit_free[C_ + e], 1)

            def half_gate(n, k):
                return dve.tensor_scalar(gate[k][:, :], mod[:, GT[n]:GT[n] + KD], 0.5, None, mul)

            up("ffn1", 0, True)
            dve.wait_ge(unit_free[C_], at["ffn1.down0"].unit[C_])
            own.then(half_gate(0, 0))
            down("ffn1.down0", gate[0][:, :])
            up("ffn1", 1, True)
            dve.wait_ge(unit_free[C_], at["ffn1.down1"].unit[C_])
            own.then(derive_scale(1))
            own.then(derive_scale(2))
            own.then(half_gate(2, 1))
            down("ffn1.down1", gate[0][:, :])
            up("ffn1", 2, False)
            dve.wait_ge(g_ready, at["ffn1.down2"].g)
            own.then(dve.memset(s1[:, :], 0.0))
            down("ffn1.down2", gate[0][:, :], 1)
            norm(1, at["norm1"].h)

            lr, li = lam[:, 0, :], lam[:, 1, :]
            Q = [x[:, :] for x in q]

            def tt(out_, x, y, op):
                own.then(dve.tensor_tensor(out_, x, y, op))

            def ts(out_, x, c0, c1, op0, op1=None):
                if op1 is None:
                    own.then(dve.tensor_scalar(out_, x, c0, None, op0))
                else:
                    own.then(dve.tensor_scalar(out_, x, c0, c1, op0, op1))

            dve.wait_ge(trig_act, 1)
            dve.tensor_tensor(Q[0], lr, dt_[:, :], mul).then_inc(trig, 1)
            tt(Q[1], li, dt_[:, :], mul)
            ts(Q[2], Q[1], 1.0 / (2 * PI), ROUND, mul, add)
            ts(Q[2], Q[2], ROUND, None, sub)
            for part in TWO_PI:
                own.then(dve.scalar_tensor_tensor(out=Q[1], in0=Q[2], scalar=-part, in1=Q[1], op0=mul, op1=add))
            ts(Q[1], Q[1], 3.1415925, -3.1415925, ALU.min, ALU.max)
            ts(Q[6], Q[1], -1.0, None, mul)
            tt(Q[6], Q[6], Q[1], ALU.max)
            dve.tensor_scalar(Q[2], Q[6], -1.0, PI / 2, mul, add).then_inc(trig, 1)
            dve.wait_ge(trig_act, 4)
            tt(pw[:, 0, 1, :], Q[3], Q[5], mul)
            tt(pw[:, 1, 1, :], Q[3], Q[4], mul)
            own.then(dve.memset(pw[:, 0, 0, :], 1.0))
            own.then(dve.memset(pw[:, 1, 0, :], 0.0))

            def cmul(dst, x, y, t0, t1):
                tt(t0, x[0], y[0], mul)
                tt(t1, x[1], y[1], mul)
                tt(dst[0], t0, t1, sub)
                tt(t0, x[0], y[1], mul)
                tt(t1, x[1], y[0], mul)
                tt(dst[1], t0, t1, add)

            for half in (1, 2, 4):
                src = [pw[:, part, 1:half + 1, :] for part in range(2)]
                by = [pw[:, part, half:half + 1, :].to_broadcast([P, half, KP]) for part in range(2)]
                dst = [pw[:, part, half + 1:2 * half + 1, :] for part in range(2)]
                t0, t1 = (tmp[:, x, 0:half * KP].rearrange("p (d k) -> p d k", k=KP) for x in range(2))
                cmul(dst, src, by, t0, t1)
            for j in range(J):
                own.then(dve.tensor_copy(pv[:, :, j, :], pw[:, :, J - 1 - j, :]))
            for l in range(LEVELS):
                if l == 0:
                    for part in range(2):
                        own.then(dve.tensor_copy(lv[:, 0, part, :], pw[:, part, 8, :]))
                else:
                    prev = [lv[:, l - 1, part, :] for part in range(2)]
                    cmul([lv[:, l, part, :] for part in range(2)], prev, prev, Q[6], Q[7])
            ts(lv[:, :, 2, :], lv[:, :, 1, :], -1.0, None, mul)
            tt(Q[0], lr, lr, mul)
            tt(Q[1], li, li, mul)
            tt(Q[0], Q[0], Q[1], add)
            own.then(dve.reciprocal(Q[0], Q[0]))
            ts(Q[1], pw[:, 0, 1, :], 1.0, None, sub)
            ai = pw[:, 1, 1, :]
            tt(Q[2], Q[1], lr, mul)
            tt(Q[3], ai, li, mul)
            tt(Q[2], Q[2], Q[3], add)
            tt(Q[2], Q[2], Q[0], mul)
            tt(Q[3], ai, lr, mul)
            tt(Q[4], Q[1], li, mul)
            tt(Q[3], Q[3], Q[4], sub)
            tt(Q[3], Q[3], Q[0], mul)
            dve.wait_ge(b_loaded, 64)
            wide = [x.rearrange("p (k o) -> p k o", o=1).to_broadcast([P, KP, H]) for x in (Q[2], Q[3])]
            t0, t1 = (tmp[:, x, 0:KP * H].rearrange("p (k h) -> p k h", h=H) for x in range(2))
            cmul([b_bar[:, part, :, :] for part in range(2)], [b_in[:, part, :, :] for part in range(2)], wide, t0, t1)
            dve.wait_ge(x_kept_done, 16)
            own.then(dve.memset(sc_a[:, :, :, :], 0.0))
            own.then(dve.memset(sc_b[:, :, :, :], 0.0))
            dve.memset(toep[:, :, :], 0.0).then_inc(toep_clear, 1)
            dve.wait_ge(ssm_full, 1)
            own.then(dve.tensor_copy(c_mat[:, :, :, :].rearrange("p r k h -> p (r k h)"), unit[C_][:, 0:2 * KP * H]))
            dve.sem_inc(unit_free[C_], 1)

            def batch(t):
                dve.wait_ge(ssm_full, 1 + 4 * t)
                four = "p d (t k) -> p t k d"
                powers = [pw[:, part, :, :].rearrange(four, k=4)[:, t, :, :] for part in range(2)]
                late = [pv[:, part, :, :].rearrange(four, k=4)[:, t, :, :] for part in range(2)]
                bb = [b_bar[:, part, :, :].rearrange("p (t k) h -> p t k h", k=4)[:, t, :, :] for part in range(2)]
                cc = [c_mat[:, part, :, :].rearrange("p (t k) h -> p t k h", k=4)[:, t, :, :] for part in range(2)]
                for part in range(2):
                    own.then(dve.tensor_copy(b_now[:, :, part, :], bb[part]))

                def product(dst, powers_, x, n, conjugate):
                    (pr, pi), (xr_, xi) = ([y.rearrange("p k (d o) -> p k d o", o=1).to_broadcast([P, 4, n, H])
                                            for y in powers_],
                                           [y.rearrange("p k (o h) -> p k o h", o=1).to_broadcast([P, 4, n, H]) for y in x])
                    t0, t1 = (tmp[:, y, 0:4 * n * H].rearrange("p (k d h) -> p k d h", k=4, h=H) for y in range(2))
                    tt(t0, pr, xr_, mul)
                    tt(t1, pi, xi, mul)
                    tt(dst[:, :, 0, :, :], t0, t1, sub)
                    tt(t0, pr, xi, mul)
                    tt(t1, pi, xr_, mul)
                    if conjugate:
                        own.then(dve.scalar_tensor_tensor(out=dst[:, :, 1, :, :], in0=t0, scalar=-1.0, in1=t1,
                                                          op0=mul, op1=sub))
                    else:
                        tt(dst[:, :, 1, :, :], t0, t1, add)

                product(ba, late, bb, J, False)
                product(ca, powers, cc, J + 1, True)
                dve.sem_inc(ba_ready, 1)

                dve.wait_ge(ssm_full, 4 + 4 * t)
                own.then(dve.tensor_copy(
                    sc_a[:, :, :, PAD + 1:PAD + C].rearrange("p k r c -> p (k r) c"),
                    unit[C_][:, :].rearrange("p (n c) -> p n c", c=C)[:, :, 0:C - 1]))
                dve.sem_inc(unit_free[C_], 1)
                n = 0
                for pair in range(2):
                    for l in range(LEVELS):
                        src, dst = ((sc_a, sc_b), (sc_b, sc_a))[l % 2]
                        off = 1 << l
                        now, then = slice(PAD, PAD + C), slice(PAD - off, PAD + C - off)
                        for to, from_, x, plus in ((0, 0, 0, src), (1, 1, 0, src), (0, 1, 2, dst), (1, 0, 1, dst)):
                            for kk in (2 * pair, 2 * pair + 1):
                                by = lv[:, l, x, :].rearrange("p (t k) -> p t k", k=4)[:, t, kk:kk + 1]
                                if n >= 2:
                                    dve.wait_ge(scan_step, 4 * 4 * LEVELS * t + n - 1)
                                dve.scalar_tensor_tensor(
                                    out=dst[:, kk, to, now], in0=src[:, kk, from_, then], scalar=by,
                                    in1=plus[:, kk, to, now], op0=mul, op1=add).then_inc(scan_step, 1)
                                n += 1
                dve.wait_ge(scan_step, 4 * 4 * LEVELS * (t + 1))
                dve.sem_inc(scan_done, 1)

            with dve.Fori(0, NT) as t:
                own.enter(t, 2 + 12 + 1)
                batch(t)
            own.leave(NT)

            dve.wait_ge(y_loaded, 16 * NT)
            for t in range(NT):
                dve.scalar_tensor_tensor(out=u_all[:, t, :], in0=u_all[:, t, :], scalar=vt[:, DS + t:DS + t + 1],
                                         in1=y_all[:, t, :], op0=mul, op1=add).then_inc(s_sum, 1)

            def s_low_part(t, before):
                dve.wait_ge(s_split, before + t + 1)
                dve.tensor_tensor(s_low[:, t, :], u_all[:, t, :], s_high[:, t, :].bitcast(F32), sub).then_inc(s_ready, 1)

            for t in range(NT):
                s_low_part(t, 0)
            own.then(dve.memset(gv[:, 0:2, 0:1], 0.0))

            def conv_in(name, m0):
                here = at[name]
                with dve.Fori(0, 4) as m:
                    own.enter(m, 4)
                    dve.wait_ge(unit_free[A_], here.unit[A_] + m + 1)
                    dve.wait_ge(slab_used, here.slab + 3 * m + 2)
                    dve.tensor_tensor(gv[:, 2:, :].rearrange("p j c -> p (j c)"), s0[:, :], unit[B_][:, :],
                                      mul).then_inc(unit_free[B_], 1)
                    dve.wait_ge(unit_free[B_], here.unit[B_] + m + 1)
                    own.then(dve.tensor_copy(gv[:, 0:2, 1:C], gv[:, J:J + 2, 0:C - 1]))

                    def tap(k):
                        return column(vt[:, CW + k * KD + m0:CW + k * KD + m0 + 4], m)

                    def steps(j):
                        return gv[:, j:j + J, :].rearrange("p j c -> p (j c)")

                    own.then(dve.tensor_scalar(taps[:, :], steps(2), tap(2), None, mul))
                    for k in (1, 0):
                        own.then(dve.scalar_tensor_tensor(out=taps[:, :], in0=steps(k), scalar=tap(k),
                                                          in1=taps[:, :], op0=mul, op1=add))
                    dve.wait_ge(slab_used, here.slab + 3 * m + 3)
                    dve.tensor_tensor(za[:, m0:m0 + 4, :][:, m, :], taps[:, :], unit[C_][:, :],
                                      mul).then_inc(unit_free[C_], 1)
                    dve.wait_ge(unit_free[C_], here.unit[C_] + m + 1)
                own.leave(4)

            conv_in("conv_in0", 0)
            here = at["glu"]
            for t in range(NT):
                dve.wait_ge(unit_free[t], here.unit[t] + 1)
                dve.tensor_tensor(u_all[:, t, :], u_all[:, t, :], stage[t % 2][:, :], mul).then_inc(gated, 1)
            for t in range(NT):
                s_low_part(t, NT)
            conv_in("conv_in1", 4)

            here = at["ssm_out"]
            with dve.Fori(0, 2) as i:
                for u in range(4):
                    m = 4 * i + u
                    dve.wait_ge(h_split, here.h + m + 1)
                    dve.tensor_tensor(h_low[:, m, :], za[:, m, :], h_high[:, m, :].bitcast(F32), sub).then_inc(h_ready, 1)
                    dve.wait_ge(h_ready, here.h + m + 1)
                    dve.wait_ge(slab_used, here.slab + 2 * i + u // 2 + 1)
                    dve.wait_ge(sg_loaded[u % 2], 16 * (2 * i + u // 2 + 1))
                    dve.tensor_tensor(mb[:, m, :], stage[u % 2][:, :], unit[u][:, :], mul).then_inc(unit_free[u], 1)
            here = at["conv_out"]
            with dve.Fori(0, KD // 2) as i:
                for e in range(2):
                    m = 2 * i + e
                    dve.wait_ge(slab_used, here.slab + m + 1)
                    dve.wait_ge(sg_loaded[e], 16 * (4 + i + 1))
                    dve.tensor_tensor(merged[:, :], stage[e][:, :], unit[e][:, :], mul).then_inc(unit_free[e], 1)
                    dve.wait_ge(unit_free[e], here.unit[e] + i + 1)
                    dve.tensor_tensor(merged[:, :], merged[:, :], mb[:, m, :], add).then_inc(merged_done, 1)
                    dve.wait_ge(g_split, here.g + m + 1)
                    dve.tensor_tensor(g_low[:, m, :], merged[:, :], g_high[:, m, :].bitcast(F32), sub).then_inc(g_ready, 1)
                    dve.wait_ge(g_ready, here.g + m + 1)
            dve.wait_ge(x_back, 16 * KD)
            own.then(dve.memset(s1[:, :], 0.0))
            down("w_out", mod[:, GT[1]:GT[1] + KD], 2)
            norm(2, at["norm2"].h)
            for n in range(3):
                up("ffn2", n, False)
                down(f"ffn2.down{n}", gate[1][:, :])
            for m in range(0, KD, 2):
                dve.wait_ge(out_full, m + 1)
                dve.tensor_copy(o_rows[:, :, m * P:(m + 1) * P],
                                unit[A_][:, :].rearrange("p (j n) -> p j n", n=P)).then_inc(unit_free[A_], 1)
            dve.wait_ge(root_done, 7)
            own.then(dve.reciprocal(rms[:, :], rms[:, :]))
            dve.wait_ge(gf_loaded, 16)
            for j in range(J):
                dve.scalar_tensor_tensor(out=o_out[:, j, :], in0=o_rows[:, j, :], scalar=rms[:, j:j + 1],
                                         in1=gf_row[:, :], op0=mul, op1=mul).then_inc(o_final, 1)


_INS = ['x', 'c', 'w_ada', 'b_ada', 'g_ffn1', 'w1_a', 'w3_a', 'w2_a', 'g_mix', 'w_in', 'conv_w', 'w_conv_out',
        'a_re', 'a_im', 'b_re', 'b_im', 'c_re', 'c_im', 'log_dt', 'd_skip', 'w_glu', 'w_ssm_out', 'w_out',
        'g_ffn2', 'w1_b', 'w3_b', 'w2_b', 'g_final']


def kernel(**inputs):
    import numpy as _np
    import concourse.bacc as _bacc
    from concourse import mybir as _mybir
    from concourse.bass_utils import run_bass_kernel_spmd as _run

    nc = _bacc.Bacc("TRN2", target_bir_lowering=False, num_devices=1, dynamic_dma_scratch_size=1024)
    arrays, args = {}, {}
    for name in _INS:
        v = _np.ascontiguousarray(inputs[name])
        arrays[f"in_{name}"] = v
        args[name] = nc.dram_tensor(f"in_{name}", v.shape, _mybir.dt.from_np(v.dtype), kind="ExternalInput").ap()
    out = nc.dram_tensor("out", (1, T, D), _mybir.dt.float32, kind="ExternalOutput").ap()
    block_kernel(nc, args, out)
    r = _run(nc, [arrays], core_ids=[0])
    return r.results[0]["out"]
```

```python
from contextlib import ExitStack

import concourse.bass as bass
from concourse import mybir

F32 = mybir.dt.float32
F32R = mybir.dt.float32r
ACT = mybir.ActivationFunctionType
ALU = mybir.AluOpType

P = 128
D = 1024
T = 1024
KD = D // P
HALF = T // 2
J = 8
C = T // J
FF = 2816
FT = FF // P
FIRST_MOD = ((0, 2), (2, KD))
CHUNKS = ((0, 8), (8, 8), (16, 6))
G, H, NS = 32, 16, 64
KP = G // 2
NT = G * H // P
LEVELS = 7
PAD = C // 2
NMOD = 9 * KD
EPS = 1e-6
PI = 3.141592653589793
ROUND = 12582912.0
TWO_PI = (6.28125, 0.0019350051879882812, 3.0199159819104966e-07)

A_, B_, C_, D_ = range(4)


def phases():
    out = [("setup", 0, (2, 1, 4, 4), 0, 2 * KD)]

    def ffn(name, ada):
        for n, (_, count) in enumerate(CHUNKS):
            c = count if ada and n < 2 else 0
            out.append((f"{name}.up{n}", 2 * count, (count, count, c, 0), count, 0))
            out.append((f"{name}.down{n}", KD, (0, 0, 4, 4), 0, 0))

    ffn("ffn1", True)
    out.append(("norm1", 0, (1, 0, 0, 0), 0, 2 * KD))
    out.append(("u", NT, (2, 2, 1, 0), 0, 0))
    out.append(("gates", 16, (8, 8, 8, 8), 0, 0))
    out.append(("conv_in0", 12, (4, 4, 4, 0), 0, 0))
    out.append(("glu", 4, (1, 1, 1, 1), 0, 0))
    out.append(("conv_in1", 12, (4, 4, 4, 0), 0, 0))
    out.append(("ssm_out", 4, (2, 2, 2, 2), 0, KD))
    out.append(("conv_out", KD, (4, 4, 0, 0), KD, 0))
    out.append(("w_out", KD, (0, 0, 4, 4), 0, 0))
    out.append(("norm2", 0, (1, 0, 0, 0), 0, 2 * KD))
    ffn("ffn2", False)
    out.append(("end", 0, (0, 0, 0, 0), 0, 0))
    return out


class At:

    def __init__(self, slab, unit, g, h):
        self.slab, self.unit, self.g, self.h = slab, unit, g, h


def starts():
    at, slab, unit, g, h = {}, 0, [0, 0, 0, 0], 0, 0
    for name, slabs, units, gs, hs in phases():
        at[name] = At(slab, tuple(unit), g, h)
        slab, g, h = slab + slabs, g + gs, h + hs
        unit = [a + b for a, b in zip(unit, units)]
    return at


ACC = {n: 2 * n + 2 * (KD - 1) * (n - 1) for n in (1, 2, 3)}


def column(ap, m):
    return ap.rearrange("p (m o) -> p m o", o=1)[:, m, :]


def by_act(j):
    return j % 3 == 1


class Steps:

    def __init__(self, engine, semaphore):
        self.engine, self.semaphore, self.base, self.k = engine, semaphore, 0, 0

    def then(self, instruction):
        instruction.then_inc(self.semaphore, 1)
        self.k += 1
        self.engine.wait_ge(self.semaphore, self.base + self.k)

    def enter(self, i, each):
        self.start = self.base + self.k
        self.base, self.k, self.each = self.start + i * each, 0, each

    def leave(self, turns):
        assert self.k == self.each, (self.k, self.each)
        self.base, self.k = self.start + turns * self.each, 0


def block_kernel(nc, a, out):
    at = starts()
    with ExitStack() as ctx:
        base = (nc.sbuf_base + 31) // 32 * 32
        top = [base]

        def region(nbytes):
            at_ = top[0]
            top[0] += nbytes
            return at_

        KB = 1024
        rX, rH, rM, rA = region(32 * KB), region(64 * KB), region(64 * KB), region(16 * KB)
        rRaw, rW, rS = region(16 * KB), region(16 * KB), region(8 * KB)

        def sb(name, shape, offset, dt=F32):
            return nc.alloc_sbuf_tensor_at(name, shape, dt, offset=offset)

        raw = sb("raw", [P, 4, KD, P], rRaw)
        w_high = sb("w_high", [P, 2, KD, P], rW, F32R)
        w_low = sb("w_low", [P, 2, KD, P], rW + 8 * KB, F32R)
        x_res = sb("x_res", [P, KD, T], rX)
        h_high = sb("h_high", [P, KD, T], rH, F32R)
        h_low = sb("h_low", [P, KD, T], rH + 32 * KB, F32R)
        g_high = sb("g_high", [P, KD, T], rM, F32R)
        g_low = sb("g_low", [P, KD, T], rM + 32 * KB, F32R)
        s0 = sb("s0", [P, T], rS)
        s1 = sb("s1", [P, T], rS + 4 * KB)
        stage = (s0, s1)
        x_rows = sb("x_rows", [P, J, D], rH)
        ada_first = sb("ada_first", [P, KD, 16 * P], rM)
        ada_first_sum = sb("ada_first_sum", [P, 16 * P], rH + 56 * KB)
        ada_raw = sb("ada_raw", [P, KD, 4 * P], rA)
        sq = sb("sq", [P, KD, HALF], rA)
        rstd = [sb(f"rstd{n}", [P, T], where) for n, where in enumerate((rM, rA, rA))]
        xr = [sb(f"xr{n}", [P, 4, HALF], where + 4 * KB)
              for n, where in enumerate((rM, rA, rA))]
        u_all = sb("u_all", [P, NT, T], rM)
        y_all = sb("y_all", [P, NT, T], rM + 16 * KB)
        s_high = sb("s_high", [P, NT, T], rM + 32 * KB, F32R)
        s_low = sb("s_low", [P, NT, T], rM + 48 * KB, F32R)
        y_chunk = sb("y_chunk", [P, 8, C], rM + 32 * KB)
        c_rows = sb("c_rows", [H, 2, KP, P], rH + 48 * KB)
        ca = sb("ca", [P, 4, 2, 9, H], rX)
        xt = sb("xt", [P, 4, 2, P], rX + 4608)
        toep = sb("toep", [P, 8, P], rX + 8704)
        sc_a = sb("sc_a", [P, 4, 2, PAD + C], rX + 12800)
        sc_b = sb("sc_b", [P, 4, 2, PAD + C], rX + 18944)
        u_chunk = sb("u_chunk", [P, 8, C], rX + 25088)
        ba = sb("ba", [P, 4, 2, J, H], rA)
        k_rows = sb("k_rows", [H, 8, P], rA + 4 * KB)
        b_now = sb("b_now", [P, 4, 2, H], rA + 8 * KB)
        za = sb("za", [P, KD, T], rX)
        gv = sb("gv", [P, J + 2, C], rA)
        taps = sb("taps", [P, T], rA + 5 * KB)
        mb = sb("mb", [P, KD, T], rX)
        merged = sb("merged", [P, T], rA)
        o_rows = sb("o_rows", [P, J, D], rH)
        o_out = sb("o_out", [P, J, D], rH + 32 * KB)
        y_gain = sb("y_gain", [P, 2, T], rA)
        rms = sb("rms", [P, J], rA + 8 * KB)

        def small(name, shape, dt=F32):
            size = 4
            for n in shape[1:]:
                size *= n
            return sb(name, shape, region((size + 31) // 32 * 32), dt)

        ident = small("ident", [P, P])
        ones = small("ones", [P, P])
        v_rows = small("v_rows", [P, P])
        e_rows = small("e_rows", [NT + KD, P])
        vt = small("vt", [P, P + NT + KD])
        cond = small("cond", [P, KD])
        mod = small("mod", [P, NMOD])
        scale = [small(f"scale{n}", [P, KD]) for n in range(3)]
        gate = [small(f"gate{n}", [P, KD]) for n in (0, 2)]
        eps = small("eps", [P, 1])
        table = small("table", [P, 1])
        ada_sum = small("ada_sum", [P, 4 * P])
        lam = sb("lam", [P, 2, KP], rM + 52 * KB)
        dt_ = sb("dt_", [P, KP], rM + 52 * KB + 128)
        q = [sb(f"q{n}", [P, KP], rM + 52 * KB + 192 + 64 * n) for n in range(8)]
        b_in = sb("b_in", [P, 2, KP, H], rM + 53 * KB)
        pv = sb("pv", [P, 2, J, KP], rM + 55 * KB)
        tmp = sb("tmp", [P, 2, 4 * 9 * H], rM + 59 * KB)
        pw = sb("pw", [P, 2, 9, KP], rA + 9 * KB)
        lv = sb("lv", [P, LEVELS, 3, KP], rA + 9 * KB + 1152)
        b_bar = sb("b_bar", [P, 2, KP, H], rA + 9 * KB + 2496)
        c_mat = sb("c_mat", [P, 2, KP, H], rA + 9 * KB + 4544)
        assert top[0] <= nc.sbuf_usable_end, top[0]
        B_ADA, GN, CW, DS, GF = 8, (80, 88, 96), 104, P, P + NT
        SH, SC, GT = (0, 24, 48), (8, 32, 56), (16, 40, 64)

        unit = [ctx.enter_context(nc.psum_tensor(f"unit_{x}", [P, T], F32)) for x in "abcd"]

        x_kept = nc.dram_tensor("x_kept", (P, KD * T), F32).ap()
        u_kept = nc.dram_tensor("u_kept", (NT, P, T), F32).ap()
        y_kept = nc.dram_tensor("y_kept", (NT, P, T), F32).ap()
        sg_kept = nc.dram_tensor("sg_kept", (16, P, T), F32).ap()

        def sem(name):
            return ctx.enter_context(nc.semaphore(name))

        slab_loaded = [sem(f"slab_loaded{r}") for r in range(4)]
        high_split = sem("high_split")
        slab_split = sem("slab_split")
        slab_half = sem("slab_half")
        slab_used = sem("slab_used")
        unit_free = [sem(f"unit_free_{x}") for x in "abcd"]
        rows_loaded = sem("rows_loaded")
        x_loaded = [sem(f"x_loaded{j}") for j in range(J)]
        ada_loaded = [sem(f"ada_loaded{k}") for k in range(KD)]
        ada_more = sem("ada_more")
        ada_summed = sem("ada_summed")
        consts = sem("consts")
        setup_full = sem("setup_full")
        vt_ready = sem("vt_ready")
        cond_ready = sem("cond_ready")
        ada_full = sem("ada_full")
        x_final = sem("x_final")
        sq_done = sem("sq_done")
        sq_used = sem("sq_used")
        acc_done = sem("acc_done")
        stat_full = sem("stat_full")
        mod_done = sem("mod_done")
        root_done = sem("root_done")
        xr_done = sem("xr_done")
        h_split = sem("h_split")
        h_ready = sem("h_ready")
        g_split = sem("g_split")
        g_ready = sem("g_ready")
        x_kept_done = sem("x_kept_done")
        lam_loaded = sem("lam_loaded")
        b_loaded = sem("b_loaded")
        c_loaded = sem("c_loaded")
        u_kept_done = [sem("u_kept_done0"), sem("u_kept_done1")]
        trig = sem("trig")
        trig_act = sem("trig_act")
        ba_ready = sem("ba_ready")
        ssm_full = sem("ssm_full")
        u_loaded = sem("u_loaded")
        toep_loaded = sem("toep_loaded")
        toep_clear = sem("toep_clear")
        scan_step = sem("scan_step")
        scan_done = sem("scan_done")
        sg_saved = [sem("sg_saved0"), sem("sg_saved1")]
        sg_loaded = [sem("sg_loaded0"), sem("sg_loaded1")]
        y_saved = sem("y_saved")
        y_loaded = sem("y_loaded")
        s_sum = sem("s_sum")
        s_split = sem("s_split")
        s_ready = sem("s_ready")
        gated = sem("gated")
        merged_done = sem("merged_done")
        x_back = sem("x_back")
        y_gained = sem("y_gained")
        out_full = sem("out_full")
        rms_ready = sem("rms_ready")
        o_final_act = sem("o_final_act")
        o_final_dve = sem("o_final_dve")
        stored = sem("stored")
        act_step = sem("act_step")
        dve_step = sem("dve_step")

        block = ctx.enter_context(nc.Block())

        @block.sync
        def _(sp):
            def row(dst, src, first):
                n = src.shape[0]
                sp.dma_start(dst[first:first + n, :], src).then_inc(rows_loaded, 16)

            def tiles(ap):
                return ap.rearrange("(m p) -> m p", p=P)

            row(v_rows, tiles(a["c"][0]), 0)
            row(v_rows, tiles(a["b_ada"][0]), B_ADA)
            for n, name in enumerate(("g_ffn1", "g_mix", "g_ffn2")):
                row(v_rows, tiles(a[name][0]), GN[n])
            row(v_rows, a["conv_w"][0].rearrange("k (m p) -> (k m) p", p=P), CW)
            row(e_rows, tiles(a["d_skip"][0]), 0)
            row(e_rows, tiles(a["g_final"]), NT)
            x_tok = a["x"][0].rearrange("(c j) n -> c j n", j=J)
            for j in range(J):
                sp.dma_start(x_rows[:, j, :], x_tok[:, j, :]).then_inc(x_loaded[j], 16)
            ada = a["w_ada"][0].rearrange("(k p) n -> p k n", p=P)
            for k in range(KD):
                if k == KD - 2:
                    for r, w in enumerate((a["w1_a"][0], a["w3_a"][0])):
                        sp.dma_start(raw[:, r, :, :], w.rearrange("(k p) (f n) -> p k f n", p=P, n=P)[:, :, 0, :]).then_inc(
                            slab_loaded[r], 16)
                sp.dma_start(ada_first[:, k, :], ada[:, k, 0:16 * P]).then_inc(ada_loaded[k], 16)

            def load(s, r, src, tiles_k=KD):
                if not (isinstance(s, int) and s < 4):
                    sp.wait_ge(slab_split, 2 * (s - 3))
                sp.dma_start(raw[:, r, 0:tiles_k, :], src).then_inc(slab_loaded[r], 16)

            def ffn(name, w1, w3, w2, with_ada):
                v1 = w1.rearrange("(k p) (f n) -> p k f n", p=P, n=P)
                v3 = w3.rearrange("(k p) (f n) -> p k f n", p=P, n=P)
                v2 = w2.rearrange("(k p) (m n) -> p k m n", p=P, n=P)
                for n, (f0, count) in enumerate(CHUNKS):
                    here = at[f"{name}.up{n}"].slab
                    many = (4, 3, 0)[n] if with_ada else 0

                    def up(i, e0=0):
                        for e in range(e0, 2):
                            load(here + 4 * i + 2 * e, 2 * e, v1[:, :, f0 + 2 * i + e, :])
                            load(here + 4 * i + 2 * e + 1, 2 * e + 1, v3[:, :, f0 + 2 * i + e, :])
                        if many:
                            first, turn0 = ((16, 0), (48, 8))[n]
                            cols = ada[:, :, first * P:(first + many * count) * P].rearrange(
                                "p k (i m) -> p k i m", m=many * P)
                            for e in range(2):
                                sp.wait_ge(ada_summed, turn0 + 1 + 2 * i + e)
                                sp.dma_start(ada_raw[:, :, 0:many * P], cols[:, :, 2 * i + e, :]).then_inc(ada_more, 16)

                    up(0, 1 if with_ada and n == 0 else 0)
                    with sp.Fori(1, count // 2) as i:
                        up(i)
                    here2 = at[f"{name}.down{n}"].slab
                    with sp.Fori(0, KD // 4) as i:
                        for r in range(4):
                            load(here2 + 4 * i + r, r, v2[:, f0:f0 + count, 4 * i + r, :], count)

            ffn("ffn1", a["w1_a"][0], a["w3_a"][0], a["w2_a"][0], True)

            w_in = a["w_in"][0].rearrange("(k p) (m n) -> p k m n", p=P, n=P)
            for r in range(NT):
                load(at["u"].slab + r, r, w_in[:, :, 24 + r, :])
            for first, where in ((36, 0), (28, 8)):
                with sp.Fori(0, 2) as i:
                    for r in range(4):
                        load(at["gates"].slab + where + 4 * i + r, r, w_in[:, :, first + 4 * i + r, :])

            def conv_in(name, m0):
                n = 0
                for m in range(m0, m0 + 4):
                    for col in (8, 16, 0):
                        load(at[name].slab + n, n % 4, w_in[:, :, col + m, :])
                        n += 1

            conv_in("conv_in0", 0)
            glu = a["w_glu"][0].rearrange("(k p) (m n) -> p k m n", p=P, n=P)
            for r in range(NT):
                load(at["glu"].slab + r, r, glu[:, :, r, :], NT)
            conv_in("conv_in1", 4)
            w_so = a["w_ssm_out"][0].rearrange("(k p) (m n) -> p k m n", p=P, n=2 * P)
            for r in range(4):
                sp.wait_ge(slab_split, 2 * (at["ssm_out"].slab + r - 3))
                sp.dma_start(raw[:, r, :, :].rearrange("p (k e) n -> p k (e n)", e=2),
                             w_so[:, :, r, :]).then_inc(slab_loaded[r], 16)
            for name, w in (("conv_out", a["w_conv_out"][0]), ("w_out", a["w_out"][0])):
                v = w.rearrange("(k p) (m n) -> p k m n", p=P, n=P)
                with sp.Fori(0, 2) as i:
                    for r in range(4):
                        load(at[name].slab + 4 * i + r, r, v[:, :, 4 * i + r, :])
            ffn("ffn2", a["w1_b"][0], a["w3_b"][0], a["w2_b"][0], False)
            out_tok = out[0].rearrange("(c j) n -> c j n", j=J)
            for j in range(J):
                if by_act(j):
                    sp.wait_ge(o_final_act, sum(by_act(n) for n in range(j + 1)))
                else:
                    sp.wait_ge(o_final_dve, sum(not by_act(n) for n in range(j + 1)))
                sp.dma_start(out_tok[:, j, :], o_out[:, j, :]).then_inc(stored, 16)
            sp.wait_ge(stored, 16 * J)

        @block.gpsimd
        def _(pool):
            pool.memset(ident[:, :], 0.0).then_inc(consts, 1)
            pool.memset(ones[:, :], 1.0).then_inc(consts, 1)
            pool.memset(eps[:, :], EPS).then_inc(consts, 1)
            pool.wait_ge(consts, 3)
            pool.affine_select(out=ident[:, :], in_=ident[:, :], compare_op=ALU.not_equal, fill=1.0,
                               base=0, pattern=[[-1, P]], channel_multiplier=1).then_inc(consts, 1)

            one = ones[:, :].rearrange("p (o n) -> p o n", o=1).to_broadcast([P, KD // 2, P])

            def split(i, first):
                for r in range(4):
                    pool.wait_ge(slab_loaded[r], 16 * (i + 1))
                    for part in range(2):
                        rows = slice(part * KD // 2, (part + 1) * KD // 2)
                        if not first or r >= 2:
                            pool.wait_ge((slab_half, slab_used)[part], 4 * i + r - 1)
                        high = w_high[:, r % 2, rows, :]
                        pool.tensor_tensor(high, raw[:, r, rows, :], one, ALU.mult).then_inc(high_split, 1)
                        pool.wait_ge(high_split, 2 * (4 * i + r) + part + 1)
                        pool.tensor_tensor(w_low[:, r % 2, rows, :], raw[:, r, rows, :], high.bitcast(F32),
                                           ALU.subtract).then_inc(slab_split, 1)

            split(0, True)
            with pool.Fori(1, at["end"].slab // 4) as i:
                split(i, False)

        @block.tensor
        def _(pe):
            def take(u, uses):
                if not (isinstance(uses, int) and uses == 0):
                    pe.wait_ge(unit_free[u], uses)

            def product(u, slot, high, low, kts, ready=None, row=None, s=None):
                for k in range(kts):
                    if s is not None and k == KD // 2:
                        pe.wait_ge(slab_split, 2 * s + 2)
                    if ready is not None:
                        pe.wait_ge(ready[0], ready[1] + k + 1)
                    wk = k if row is None else row(k)
                    wh = w_high[:, slot, wk, :]
                    wl = w_low[:, slot, wk, :]
                    for part, (w, x) in enumerate(((wh, high), (wh, low), (wl, high))):
                        for half in range(2):
                            t = slice(512 * half, 512 * half + 512)
                            last = pe.matmul(unit[u][:, t], w, x[:, k, t], start=(k == 0 and part == 0),
                                             stop=(k == kts - 1 and part == 2))
                    if s is not None and k == KD // 2 - 1 and kts > KD // 2:
                        last.then_inc(slab_half, 1)
                return last

            def all_used(s, last):
                last.then_inc(slab_used, 1)
                pe.wait_ge(slab_used, s + 1)
                pe.sem_inc(slab_half, 1)

            def slab(s, slot, u, uses, high, low, kts, ready=None):
                pe.wait_ge(slab_split, 2 * s + 1)
                take(u, uses)
                last = product(u, slot, high, low, kts, ready=ready, s=s)
                if kts > KD // 2:
                    last.then_inc(slab_used, 1)
                else:
                    all_used(s, last)

            pe.wait_ge(consts, 4)
            pe.wait_ge(rows_loaded, 8 * 16)
            pe.transpose(unit[A_][:, 0:P], v_rows[:, :], ident[:, :])
            pe.transpose(unit[A_][:, P:P + NT + KD], e_rows[:, :], ident[0:NT + KD, 0:NT + KD]).then_inc(setup_full, 1)
            for j in range(J):
                pe.wait_ge(x_loaded[j], 16)
                u, uses = (C_, D_)[j % 2], j // 2
                take(u, uses)
                for m in range(KD):
                    last = pe.transpose(unit[u][:, m * P:(m + 1) * P], x_rows[:, j, m * P:(m + 1) * P], ident[:, :])
                last.then_inc(setup_full, 1)

            def ada_tiles(w, count, u):
                for t in range(count):
                    last = pe.matmul(unit[u][:, t:t + 1], w[:, t * P:(t + 1) * P], ones[:, 0:1], start=True, stop=True)
                last.then_inc(ada_full, 1)

            def statistics(n, uses):
                take(A_, uses)
                for half in range(2):
                    t = slice(HALF * half, HALF * half + HALF)
                    if n == 0:
                        for m in range(KD):
                            pe.wait_ge(sq_done, KD * half + m + 1)
                            pe.matmul(unit[A_][:, t], ones[:, :], sq[:, m, :], start=(m == 0),
                                      stop=(m == KD - 1)).then_inc(sq_used, 1)
                    else:
                        pe.wait_ge(acc_done, ACC[n] + 2 * (KD - 2) + half + 1)
                        pe.matmul(unit[A_][:, t], ones[:, :], s1[:, t], start=True, stop=False)
                        pe.wait_ge(sq_done, 2 * KD * n + 2 * (KD - 1) + half + 1)
                        pe.matmul(unit[A_][:, t], ones[:, :], s0[:, t], start=False, stop=True).then_inc(stat_full, 1)

            statistics(0, 1)
            pe.wait_ge(ada_summed, 1)
            take(B_, 0)
            for part, (k0, k1) in enumerate(FIRST_MOD):
                for t in [*range(k0, k1), *range(KD + k0, KD + k1)]:
                    last = pe.matmul(unit[B_][:, HALF * part + t:HALF * part + t + 1],
                                     ada_first_sum[:, t * P:(t + 1) * P], ones[:, 0:1], start=True, stop=True)
                last.then_inc(ada_full, 1)

            def first_pair(s, uses, h0):
                pe.wait_ge(slab_split, 2 * s + 3)
                for u in (A_, B_):
                    take(u, uses[u])
                for half in range(2):
                    t = slice(HALF * half, HALF * half + HALF)
                    for k in range(KD):
                        pe.wait_ge(h_ready, h0 + KD * half + k + 1)
                        if half == 0 and k == KD // 2:
                            pe.wait_ge(slab_split, 2 * s + 4)
                        for u in (A_, B_):
                            wh, wl = w_high[:, u, k, :], w_low[:, u, k, :]
                            for part, (w, x) in enumerate(((wh, h_high), (wh, h_low), (wl, h_high))):
                                last = pe.matmul(unit[u][:, t], w, x[:, k, t], start=(k == 0 and part == 0),
                                                 stop=(k == KD - 1 and part == 2))
                            if half == 1 and k == KD // 2 - 1:
                                last.then_inc(slab_half, 1)
                            if half == 1 and k == KD - 1:
                                last.then_inc(slab_used, 1)

            def up(name, n, i, with_ada):
                here = at[f"{name}.up{n}"]
                if isinstance(i, int):
                    first_pair(here.slab, here.unit, here.h - 2 * KD)
                else:
                    slab(here.slab + 2 * i, 0, A_, here.unit[A_] + i, h_high, h_low, KD)
                if with_ada and n < 2:
                    pe.wait_ge(ada_summed, 8 * n + i + 2)
                    take(C_, here.unit[C_] + i)
                    ada_tiles(ada_sum, 4 - n, C_)
                if not isinstance(i, int):
                    slab(here.slab + 2 * i + 1, 1, B_, here.unit[B_] + i, h_high, h_low, KD)

            def down(name, kts, i):
                here = at[name]
                for e in range(2):
                    slab(here.slab + 2 * i + e, e, C_ + e, here.unit[C_ + e] + i, g_high, g_low, kts,
                         (g_ready, here.g - kts))

            ends = at["end"]

            def back(m, i, e):
                pe.wait_ge(y_gained, m + 1)
                take(e, ends.unit[e] + i)
                for j in range(J):
                    last = pe.transpose(unit[e][:, j * P:(j + 1) * P], y_gain[:, e, j * P:(j + 1) * P], ident[:, :])
                last.then_inc(out_full, 1)

            def last_down(i, count):
                here = at["ffn2.down2"]
                for e in range(2):
                    slab(here.slab + 2 * i + e, e, C_ + e, here.unit[C_ + e] + i, g_high, g_low, count,
                         (g_ready, here.g - count))
                    if e == 1:
                        back(2 * i, i, 0)
                    elif not isinstance(i, int):
                        back(2 * i - 1, i - 1, 1)

            def ffn(name, with_ada):
                for n, (_, count) in enumerate(CHUNKS):
                    if n == 0:
                        up(name, 0, 0, with_ada)
                    with pe.Fori(1 if n == 0 else 0, count) as i:
                        up(name, n, i, with_ada)
                    if name == "ffn2" and n == 2:
                        last_down(0, count)
                        with pe.Fori(1, KD // 2) as i:
                            last_down(i, count)
                        back(KD - 1, KD // 2 - 1, 1)
                    else:
                        with pe.Fori(0, KD // 2) as i:
                            down(f"{name}.down{n}", count, i)

            ffn("ffn1", True)
            statistics(1, at["norm1"].unit[A_])

            here = at["u"]
            pe.wait_ge(c_loaded, 16 * 2)
            take(C_, here.unit[C_])
            for part in range(2):
                for k in range(KP):
                    col = (part * KP + k) * H
                    last = pe.transpose(unit[C_][:, col:col + H], c_rows[:, part, k, :], ident[0:H, 0:H])
            last.then_inc(ssm_full, 1)
            first_pair(here.slab, here.unit, here.h - 2 * KD)
            for t in range(2, NT):
                slab(here.slab + t, t % 2, t % 2, here.unit[t % 2] + t // 2, h_high, h_low, KD)

            here = at["gates"]

            def gates(t):
                def gate_slab(q_):
                    slab(here.slab + 4 * t + q_, q_ % 2, q_ % 2, here.unit[q_ % 2] + 2 * t + q_ // 2, h_high, h_low, KD)

                pe.wait_ge(ba_ready, t + 1)
                take(D_, here.unit[D_] + 2 * t)
                take(C_, here.unit[C_] + 2 * t)
                for kk in range(4):
                    for part in range(2):
                        col = (2 * kk + part) * P
                        last = pe.transpose(unit[C_][:, col:col + P],
                                            ba[:, kk, part, :, :].rearrange("p j h -> p (j h)"), ident[:, :])
                last.then_inc(ssm_full, 1)
                for g2 in range(2):
                    rows = slice(NS * g2, NS * g2 + NS)
                    for kk in range(4):
                        col = (4 * g2 + kk) * P
                        for part in range(2):
                            last = pe.matmul(unit[D_][0:H, col:col + P], b_now[rows, kk, part, :],
                                             ca[rows, kk, part, 0:8, :].rearrange("p d h -> p (d h)"),
                                             start=(part == 0), stop=(part == 1))
                last.then_inc(ssm_full, 1)
                pe.wait_ge(unit_free[C_], here.unit[C_] + 2 * t + 1)
                pe.wait_ge(u_loaded, 128 * (t + 1))
                for g2 in range(2):
                    for kk in range(4):
                        for part in range(2):
                            col = (2 * kk + part) * P
                            last = pe.matmul(unit[C_][NS * g2:NS * g2 + NS, col:col + P],
                                             xt[:, kk, part, NS * g2:NS * g2 + NS], u_chunk[:, 2 * kk + g2, :],
                                             start=True, stop=True)
                last.then_inc(ssm_full, 1)
                gate_slab(0)
                gate_slab(1)
                gate_slab(2)
                pe.wait_ge(scan_done, t + 1)
                pe.wait_ge(toep_loaded, 128 * (t + 1))
                take(D_, here.unit[D_] + 2 * t + 1)
                for g2 in range(2):
                    rows = slice(NS * g2, NS * g2 + NS)
                    for kk in range(4):
                        dst = unit[D_][:, (4 * g2 + kk) * P:(4 * g2 + kk + 1) * P]
                        pe.matmul(dst, toep[:, 4 * g2 + kk, :], u_chunk[:, 2 * kk + g2, :], start=True, stop=False)
                        for part in range(2):
                            last = pe.matmul(dst, ca[rows, kk, part, 1:9, :].rearrange("p d h -> p (d h)"),
                                             sc_b[rows, kk, part, PAD:], start=False, stop=(part == 1))
                last.then_inc(ssm_full, 1)
                gate_slab(3)

            with pe.Fori(0, NT) as t:
                gates(t)

            def conv_in(name):
                here = at[name]
                with pe.Fori(0, 2) as i:
                    for e in range(2):
                        for n, u in enumerate((A_, B_, C_)):
                            slab(here.slab + 6 * i + 3 * e + n, (3 * e + n) % 2, u, here.unit[u] + 2 * i + e,
                                 h_high, h_low, KD)

            conv_in("conv_in0")
            here = at["glu"]
            for t in range(NT):
                slab(here.slab + t, t % 2, t, here.unit[t], s_high, s_low, NT, (s_ready, 0))
            conv_in("conv_in1")
            here = at["ssm_out"]
            with pe.Fori(0, 2) as i:
                for e in range(2):
                    pe.wait_ge(slab_split, 2 * (here.slab + 2 * i + e) + 2)
                    for half in range(2):
                        u = 2 * e + half
                        take(u, here.unit[u] + i)
                        last = product(u, e, s_high, s_low, NT, ready=(s_ready, NT), row=lambda k: 2 * k + half)
                    all_used(here.slab + 2 * i + e, last)
            here = at["conv_out"]
            with pe.Fori(0, KD // 2) as i:
                for e in range(2):
                    slab(here.slab + 2 * i + e, e, e, here.unit[e] + i, h_high, h_low, KD, (h_ready, here.h - KD))
            with pe.Fori(0, KD // 2) as i:
                down("w_out", KD, i)
            statistics(2, at["norm2"].unit[A_])
            ffn("ffn2", False)

            pe.wait_ge(acc_done, ACC[3] + 2 * (KD - 1))
            pe.wait_ge(sq_done, 8 * KD)
            take(C_, ends.unit[C_])
            for j in range(J):
                t = slice(j * P, (j + 1) * P)
                pe.matmul(unit[C_][:, j:j + 1], s1[:, t], ones[:, 0:1], start=True, stop=False)
                last = pe.matmul(unit[C_][:, j:j + 1], s0[:, t], ones[:, 0:1], start=False, stop=True)
            last.then_inc(stat_full, 1)

        @block.scalar
        def _(act):
            own = Steps(act, act_step)

            act.wait_ge(vt_ready, 1)
            act.activation(cond[:, :], vt[:, 0:KD], ACT.Silu).then_inc(cond_ready, 1)

            def square(m, half, added):
                t = slice(HALF * half, HALF * half + HALF)
                act.wait_ge(acc_done, added)
                act.activation(s0[:, t], x_res[:, m, t], ACT.Square).then_inc(sq_done, 1)

            def load_sqrt():
                return act.activation(table[:, :], eps[:, :], ACT.Sqrt)

            for half in range(2):
                t = slice(HALF * half, HALF * half + HALF)
                for j in (4 * half + 1, 4 * half + 3):
                    act.wait_ge(setup_full, 2 + j)
                    act.activation(x_res[:, :, j * C:(j + 1) * C], unit[D_][:, :].rearrange("p (m c) -> p m c", c=C),
                                   ACT.Copy).then_inc(unit_free[D_], 1)
                if half == 0:
                    own.then(load_sqrt())
                act.wait_ge(unit_free[C_], 2 * half + 2)
                act.wait_ge(unit_free[D_], 2 * half + 2)
                for m in range(KD):
                    if half == 1:
                        act.wait_ge(sq_used, m + 1)
                    act.activation(sq[:, m, :], x_res[:, m, t], ACT.Square).then_inc(sq_done, 1)

            def load_parameters():
                def as_states(ap):
                    return ap.rearrange("(k g) p -> (g p) k", g=2)

                with nc.allow_non_contiguous_dma(reason="small parameter tables"):
                    act.dma_start(lam[:, 0, :], as_states(a["a_re"][0])).then_inc(lam_loaded, 16)
                    act.dma_start(lam[:, 1, :], as_states(a["a_im"][0])).then_inc(lam_loaded, 16)
                    for g2 in range(2):
                        per = a["log_dt"][0].rearrange("(k g) -> g k", g=2)[g2:g2 + 1, :]
                        act.dma_start(dt_[NS * g2:NS * g2 + NS, :], per.to_broadcast([NS, KP])).then_inc(lam_loaded, 16)
                    for part, b in enumerate(("b_re", "b_im")):
                        act.dma_start(b_in[:, part, :, :], a[b][0].rearrange("(k g) p h -> (g p) k h", g=2)).then_inc(b_loaded, 16)

            def norm(n, h0):
                for half in range(2):
                    t = slice(HALF * half, HALF * half + HALF)
                    if n == 0:
                        act.wait_ge(sq_used, KD * (half + 1))
                    else:
                        act.wait_ge(stat_full, 2 * (n - 1) + half + 1)
                    act.activation(s0[:, t], unit[A_][:, t], ACT.Sqrt, bias=eps[:, 0:1],
                                   scale=1.0 / D).then_inc(root_done, 1)
                if n == 1:
                    load_parameters()
                    act.dma_start(x_kept, x_res[:, :, :].rearrange("p k t -> p (k t)")).then_inc(x_kept_done, 16)
                for step in range(2 * KD):
                    half, m = divmod(step, KD)
                    t = slice(HALF * half, HALF * half + HALF)
                    tile = xr[n][:, step % 4, :]
                    act.wait_ge(xr_done, 2 * KD * n + step + 1)
                    for part, (k0, _) in enumerate(FIRST_MOD):
                        if n == 0 and step == k0:
                            act.wait_ge(mod_done, part + 1)
                    own.then(act.activation(tile, tile, ACT.Identity, scale=scale[n][:, m:m + 1],
                                            bias=mod[:, SH[n] + m:SH[n] + m + 1]))
                    act.activation(h_high[:, m, t], tile, ACT.Copy).then_inc(h_split, 1)

            norm(0, 0)

            def up(name, n):
                here = at[f"{name}.up{n}"]
                with act.Fori(0, CHUNKS[n][1]) as i:
                    act.wait_ge(slab_used, here.slab + 2 * i + 1)
                    act.activation(s0[:, :], unit[A_][:, :], ACT.Silu).then_inc(unit_free[A_], 1)
                    act.wait_ge(unit_free[B_], here.unit[B_] + i + 1)
                    act.activation(g_high[:, i, :], s1[:, :], ACT.Copy).then_inc(g_split, 1)

            def down_squares(n):
                with act.Fori(0, KD) as m:
                    for half in range(2):
                        act.wait_ge(x_final, 2 * KD * (n - 1) + 2 * m + half + 1)
                        square(m, half, ACC[n] + 2 * m + half - 1)

            for n in range(3):
                up("ffn1", n)
            own.then(load_sqrt())
            act.wait_ge(slab_used, at["ffn1.down2"].slab)
            with nc.allow_non_contiguous_dma(reason="rows of 256 bytes"):
                for part, c in enumerate(("c_re", "c_im")):
                    act.dma_start(c_rows[:, part, :, :].rearrange("h k (g p) -> h (k g) p", g=2),
                                  a[c][0].rearrange("g h p -> h g p")).then_inc(c_loaded, 16)
            down_squares(1)
            norm(1, at["norm1"].h)

            act.wait_ge(lam_loaded, 64)
            act.activation(dt_[:, :], dt_[:, :], ACT.Exp).then_inc(trig_act, 1)
            act.wait_ge(trig, 1)
            act.activation(q[3][:, :], q[0][:, :], ACT.Exp).then_inc(trig_act, 1)
            act.wait_ge(trig, 2)
            act.activation(q[4][:, :], q[1][:, :], ACT.Sin).then_inc(trig_act, 1)
            act.activation(q[5][:, :], q[2][:, :], ACT.Sin).then_inc(trig_act, 1)

            def load_u(t):
                if isinstance(t, int) and t == 0:
                    act.wait_ge(u_kept_done[0], 16)
                else:
                    act.wait_ge(ssm_full, 1 + 4 * t)
                u_src = u_kept.rearrange("t (g h) (j c) -> j t h g c", h=H, j=J)
                for j in range(J):
                    act.dma_start(u_chunk[H * j:H * j + H, :, :], u_src[j][t]).then_inc(u_loaded, 16)

            here = at["u"]
            for t in range(NT):
                act.wait_ge(slab_used, here.slab + t + 1)
                act.activation(u_all[:, t, :], unit[t % 2][:, :], ACT.Copy).then_inc(unit_free[t % 2], 1)
                act.wait_ge(unit_free[t % 2], here.unit[t % 2] + t // 2 + 1)
                act.dma_start(u_kept[t], u_all[:, t, :]).then_inc(u_kept_done[min(t, 1)], 16)
                if t == 1:
                    act.wait_ge(x_kept_done, 16)
                    load_u(0)
            act.wait_ge(u_kept_done[1], 16 * (NT - 1))

            here = at["gates"]

            def gates(t, first=False, last=False):
                def gate_slab(q_):
                    act.wait_ge(slab_used, here.slab + 4 * t + q_ + 1)
                    if not first or q_ >= 2:
                        act.wait_ge(sg_saved[q_ % 2], 16 * (2 * t + q_ // 2))
                    act.activation(stage[q_ % 2][:, :], unit[q_ % 2][:, :], ACT.Sigmoid).then_inc(unit_free[q_ % 2], 1)
                    act.wait_ge(unit_free[q_ % 2], here.unit[q_ % 2] + 2 * t + q_ // 2 + 1)
                    act.dma_start(sg_kept.rearrange("(t q) p n -> q t p n", q=4)[q_][t], stage[q_ % 2][:, :]).then_inc(sg_saved[q_ % 2], 16)

                act.wait_ge(ssm_full, 2 + 4 * t)
                act.activation(xt[:, :, :, :].rearrange("p a b n -> p (a b n)"), unit[C_][:, :], ACT.Copy).then_inc(unit_free[C_], 1)
                act.wait_ge(ssm_full, 3 + 4 * t)
                act.activation(k_rows[:, :, :].rearrange("h g n -> h (g n)"), unit[D_][0:H, :], ACT.Copy).then_inc(unit_free[D_], 1)
                act.wait_ge(unit_free[D_], here.unit[D_] + 2 * t + 1)
                if first:
                    act.wait_ge(toep_clear, 1)
                for j in range(J):
                    act.dma_start(toep[H * j:H * j + H, :, H * j:P], k_rows[:, :, 0:P - H * j]).then_inc(toep_loaded, 16)
                gate_slab(0)
                gate_slab(1)
                gate_slab(2)
                act.wait_ge(ssm_full, 5 + 4 * t)
                act.activation(y_chunk[:, :, :].rearrange("p (k g) c -> p g k c", g=2),
                               unit[D_][:, :].rearrange("p (g k c) -> p g k c", g=2, k=4),
                               ACT.Copy).then_inc(unit_free[D_], 1)
                act.wait_ge(unit_free[D_], here.unit[D_] + 2 * t + 2)
                y_dst = y_kept.rearrange("t (g h) (i c) -> i t h g c", h=H, i=J)
                for i in range(J):
                    act.dma_start(y_dst[i][t], y_chunk[H * i:H * i + H, :, :]).then_inc(y_saved, 16)
                if not last:
                    load_u(t + 1)
                gate_slab(3)
                act.wait_ge(y_saved, 128 * (t + 1))
                act.dma_start(y_all[:, t, :], y_kept[t]).then_inc(y_loaded, 16)

            gates(0, first=True)
            with act.Fori(1, NT - 1) as t:
                gates(t)
            gates(NT - 1, last=True)

            for t in range(NT):
                act.wait_ge(s_sum, t + 1)
                own.then(act.activation(u_all[:, t, :], u_all[:, t, :], ACT.Gelu_apprx_tanh))
                act.activation(s_high[:, t, :], u_all[:, t, :], ACT.Copy).then_inc(s_split, 1)

            def conv_in(name):
                here = at[name]
                with act.Fori(0, 4) as m:
                    act.wait_ge(slab_used, here.slab + 3 * m + 1)
                    act.wait_ge(unit_free[B_], here.unit[B_] + m)
                    act.activation(s0[:, :], unit[A_][:, :], ACT.Copy).then_inc(unit_free[A_], 1)

            for stage_ in range(2):
                act.wait_ge(sg_saved[stage_], 16 * 8)
            conv_in("conv_in0")
            here = at["glu"]
            for t in range(NT):
                act.wait_ge(slab_used, here.slab + t + 1)
                if t >= 2:
                    act.wait_ge(gated, t - 1)
                else:
                    act.wait_ge(unit_free[B_], here.unit[B_])
                act.activation(stage[t % 2][:, :], unit[t][:, :], ACT.Sigmoid).then_inc(unit_free[t], 1)
            for t in range(NT):
                act.wait_ge(gated, t + 1)
                act.activation(s_high[:, t, :], u_all[:, t, :], ACT.Copy).then_inc(s_split, 1)
            conv_in("conv_in1")

            def sg_load(n, e):
                act.dma_start(stage[e][:, :], sg_kept[n]).then_inc(sg_loaded[e], 16)

            here = at["ssm_out"]
            act.wait_ge(unit_free[B_], here.unit[B_])
            act.wait_ge(unit_free[C_], here.unit[C_])
            sg_load(0, 0)
            sg_load(1, 1)
            act.wait_ge(slab_used, here.slab)
            with act.Fori(0, 2) as i:
                for u in range(4):
                    m = 4 * i + u
                    act.activation(h_high[:, m, :], za[:, m, :], ACT.Copy).then_inc(h_split, 1)
                    act.wait_ge(unit_free[u], here.unit[u] + i + 1)
                    sg_load(m + 2, u % 2)
            here = at["conv_out"]
            x_tiles = x_kept.rearrange("p (k t) -> k p t", k=KD)
            with nc.allow_non_contiguous_dma(reason="rows of 4 KiB"):
                def conv_out(i, more):
                    for e in range(2):
                        m = 2 * i + e
                        act.wait_ge(unit_free[e], here.unit[e] + i + 1)
                        if more:
                            sg_load(m + 10, e)
                        act.wait_ge(merged_done, m + 1)
                        act.activation(g_high[:, m, :], merged[:, :], ACT.Copy).then_inc(g_split, 1)
                        act.dma_start(x_res[:, m, :], x_tiles[m]).then_inc(x_back, 16)

                with act.Fori(0, KD // 2 - 1) as i:
                    conv_out(i, True)
                conv_out(KD // 2 - 1, False)
            own.then(load_sqrt())
            down_squares(2)
            norm(2, at["norm2"].h)
            for n in range(3):
                up("ffn2", n)
            here, ends = at["ffn2.down2"], at["end"]
            with act.Fori(0, KD // 2) as i:
                for e in range(2):
                    m = 2 * i + e
                    for half in range(2):
                        act.wait_ge(x_final, 4 * KD + 2 * m + half + 1)
                        square(m, half, ACC[3] + 2 * m + half - 1)
                act.wait_ge(out_full, 2 * i + 1)
                act.activation(o_rows[:, :, :].rearrange("p j (m n) -> p m j n", n=P)[:, 2 * i, :, :],
                               unit[A_][:, :].rearrange("p (j n) -> p j n", n=P), ACT.Copy).then_inc(unit_free[A_], 1)
            act.wait_ge(stat_full, 5)
            act.activation(rms[:, :], unit[C_][:, 0:J], ACT.Sqrt, bias=eps[:, 0:1], scale=1.0 / D).then_inc(root_done, 1)
            act.wait_ge(unit_free[B_], ends.unit[B_] + 4)
            act.wait_ge(rms_ready, 1)
            for j in range(J):
                if by_act(j):
                    act.activation(o_out[:, j, :], o_rows[:, j, :], ACT.Copy, scale=rms[:, j:j + 1]).then_inc(o_final_act, 1)

        @block.vector
        def _(dve):
            own = Steps(dve, dve_step)
            mul, add, sub = ALU.mult, ALU.add, ALU.subtract

            dve.wait_ge(setup_full, 1)
            dve.tensor_copy(vt[:, :], unit[A_][:, 0:P + NT + KD]).then_inc(vt_ready, 1)
            dve.wait_ge(vt_ready, 1)
            dve.sem_inc(unit_free[A_], 1)

            for j in range(0, J, 2):
                dve.wait_ge(setup_full, 2 + j)
                dve.tensor_copy(x_res[:, :, j * C:(j + 1) * C],
                                unit[C_][:, :].rearrange("p (m c) -> p m c", c=C)).then_inc(unit_free[C_], 1)

            def accumulate(half, squared, count):
                t = slice(HALF * half, HALF * half + HALF)
                dve.wait_ge(sq_done, squared + 1)
                dve.tensor_tensor(s1[:, t], s1[:, t], s0[:, t], add).then_inc(acc_done, 1)
                dve.wait_ge(acc_done, count + 1)

            def clear_sums(n):
                for half in range(2):
                    dve.memset(s1[:, HALF * half:HALF * half + HALF], 0.0).then_inc(acc_done, 1)
                dve.wait_ge(acc_done, ACC[n])

            def root(n, half):
                t = slice(HALF * half, HALF * half + HALF)
                dve.wait_ge(root_done, 2 * n + half + 1)
                own.then(dve.reciprocal(rstd[n][:, t], s0[:, t]))

            def ada_columns(dst, src, count, loaded=None):
                for k in range(KD):
                    if loaded is not None:
                        if k == KD - 3:
                            root(0, 0)
                            root(0, 1)
                            dve.sem_inc(unit_free[A_], 1)
                        dve.wait_ge(loaded[k], 16)
                    by = cond[:, k:k + 1]
                    if k == 0:
                        last = dve.tensor_scalar(dst[:, 0:count], src[:, k, 0:count], by, None, mul)
                    else:
                        last = dve.scalar_tensor_tensor(out=dst[:, 0:count], in0=src[:, k, 0:count], scalar=by,
                                                        in1=dst[:, 0:count], op0=mul, op1=add)
                    if k < KD - 1:
                        own.then(last)
                last.then_inc(ada_summed, 1)

            dve.wait_ge(cond_ready, 1)
            ada_columns(ada_first_sum, ada_first, 16 * P, ada_loaded)
            def derive_scale(n, k0=0, k1=KD):
                return dve.scalar_tensor_tensor(out=scale[n][:, k0:k1], in0=mod[:, SC[n] + k0:SC[n] + k1], scalar=1.0,
                                                in1=vt[:, GN[n] + k0:GN[n] + k1], op0=add, op1=mul)

            def first_mod(part):
                k0, k1 = FIRST_MOD[part]
                dve.wait_ge(ada_full, part + 1)
                for first in (SH[0], SC[0]):
                    a0, a1 = first + k0, first + k1
                    own.then(dve.tensor_tensor(mod[:, a0:a1], unit[B_][:, HALF * part + a0:HALF * part + a1],
                                               vt[:, B_ADA + a0:B_ADA + a1], add))
                derive_scale(0, k0, k1).then_inc(mod_done, 1)
                dve.wait_ge(mod_done, part + 1)

            def norm(n, h0):
                def scaled(step):
                    half, m = divmod(step, KD)
                    t = slice(HALF * half, HALF * half + HALF)
                    if step >= 4:
                        dve.wait_ge(h_ready, h0 + step - 3)
                    dve.tensor_tensor(xr[n][:, step % 4, :], x_res[:, m, t], rstd[n][:, t], mul).then_inc(xr_done, 1)

                def low(step):
                    half, m = divmod(step, KD)
                    t = slice(HALF * half, HALF * half + HALF)
                    if n == 1 and step == KD // 2:
                        dve.wait_ge(ssm_full, 1)
                    dve.wait_ge(h_split, h0 + step + 1)
                    dve.tensor_tensor(h_low[:, m, t], xr[n][:, step % 4, :], h_high[:, m, t].bitcast(F32),
                                      sub).then_inc(h_ready, 1)

                if n > 0:
                    root(n, 0)
                    dve.wait_ge(root_done, 2 * n + 2)
                    dve.sem_inc(unit_free[A_], 1)
                ahead = 3
                for step in range(ahead):
                    scaled(step)
                if n == 0:
                    first_mod(0)
                for step in range(2 * KD):
                    low(step)
                    if step == 1 and n == 0:
                        first_mod(1)
                        dve.sem_inc(unit_free[B_], 1)
                    if step + ahead == KD and n > 0:
                        root(n, 1)
                    if step + ahead < 2 * KD:
                        scaled(step + ahead)
                dve.wait_ge(h_ready, h0 + 2 * KD)

            norm(0, 0)

            def up(name, n, with_ada):
                here = at[f"{name}.up{n}"]
                with_ada = with_ada and n < 2
                with dve.Fori(0, CHUNKS[n][1]) as i:
                    if with_ada:
                        first, many = ((16, 4), (48, 3))[n]
                        own.enter(i, KD - 1)
                        dve.wait_ge(ada_more, 16 * (8 * n + i + 1))
                        ada_columns(ada_sum, ada_raw, many * P)
                        cols = slice(first, first + 8 * many)
                        dve.wait_ge(ada_full, 8 * n + i + 3)
                        dve.tensor_tensor(
                            mod[:, cols].rearrange("p (i t) -> p i t", t=many)[:, i, :], unit[C_][:, 0:many],
                            vt[:, B_ADA + first:B_ADA + first + 8 * many].rearrange("p (i t) -> p i t", t=many)[:, i, :],
                            add).then_inc(unit_free[C_], 1)
                    dve.wait_ge(unit_free[A_], here.unit[A_] + i + 1)
                    dve.wait_ge(slab_used, here.slab + 2 * i + 2)
                    dve.tensor_tensor(s1[:, :], s0[:, :], unit[B_][:, :], mul).then_inc(unit_free[B_], 1)
                    dve.wait_ge(g_split, here.g + i + 1)
                    dve.tensor_tensor(g_low[:, i, :], s1[:, :], g_high[:, i, :].bitcast(F32), sub).then_inc(g_ready, 1)
                    dve.wait_ge(g_ready, here.g + i + 1)
                if with_ada:
                    own.leave(CHUNKS[n][1])

            def down(name, g, n=None):
                here = at[name]

                def tile(m, i, e):
                    dve.wait_ge(slab_used, here.slab + m + 1)
                    if n is None:
                        dve.scalar_tensor_tensor(out=x_res[:, m, :], in0=unit[C_ + e][:, :], scalar=column(g, m),
                                                 in1=x_res[:, m, :], op0=mul, op1=add).then_inc(unit_free[C_ + e], 1)
                        return
                    for half in range(2):
                        t = slice(HALF * half, HALF * half + HALF)
                        dve.scalar_tensor_tensor(out=x_res[:, m, t], in0=unit[C_ + e][:, t], scalar=column(g, m),
                                                 in1=x_res[:, m, t], op0=mul, op1=add).then_inc(x_final, 1)
                    dve.wait_ge(x_final, 2 * KD * (n - 1) + 2 * m + 2)
                    dve.sem_inc(unit_free[C_ + e], 1)
                    if n == 3:
                        if not isinstance(i, int) or i > 0:
                            dve.wait_ge(out_full, m - 1)
                        dve.tensor_scalar(y_gain[:, e, :], x_res[:, m, :], column(vt[:, GF:GF + KD], m), None,
                                          mul).then_inc(y_gained, 1)
                    if not isinstance(m, int) or m < KD - 1:
                        for half in range(2):
                            accumulate(half, 2 * KD * n + 2 * m + half, ACC[n] + 2 * m + half)

                def back(m, i):
                    dve.wait_ge(out_full, m + 1)
                    dve.tensor_copy(o_rows[:, :, :].rearrange("p j (m n) -> p m j n", n=P)[:, m, :, :],
                                    unit[B_][:, :].rearrange("p (j n) -> p j n", n=P)).then_inc(unit_free[B_], 1)

                def pair(i):
                    tile(2 * i, i, 0)
                    if n == 3 and (not isinstance(i, int) or i > 0):
                        back(2 * i - 1, i)
                    tile(2 * i + 1, i, 1)

                if n is None:
                    with dve.Fori(0, KD // 2) as i:
                        pair(i)
                else:
                    pair(0)
                    with dve.Fori(1, KD // 2 - 1) as i:
                        pair(i)
                    pair(KD // 2 - 1)
                    if n == 3:
                        back(KD - 1, KD // 2)

            def half_gate(n, k):
                return dve.tensor_scalar(gate[k][:, :], mod[:, GT[n]:GT[n] + KD], 0.5, None, mul)

            up("ffn1", 0, True)
            dve.wait_ge(unit_free[C_], at["ffn1.down0"].unit[C_])
            own.then(half_gate(0, 0))
            down("ffn1.down0", gate[0][:, :])
            up("ffn1", 1, True)
            dve.wait_ge(unit_free[C_], at["ffn1.down1"].unit[C_])
            own.then(derive_scale(1))
            own.then(derive_scale(2))
            own.then(half_gate(2, 1))
            down("ffn1.down1", gate[0][:, :])
            up("ffn1", 2, False)
            dve.wait_ge(g_ready, at["ffn1.down2"].g)
            clear_sums(1)
            down("ffn1.down2", gate[0][:, :], 1)
            norm(1, at["norm1"].h)

            lr, li = lam[:, 0, :], lam[:, 1, :]
            Q = [x[:, :] for x in q]

            def tt(out_, x, y, op):
                own.then(dve.tensor_tensor(out_, x, y, op))

            def ts(out_, x, c0, c1, op0, op1=None):
                if op1 is None:
                    own.then(dve.tensor_scalar(out_, x, c0, None, op0))
                else:
                    own.then(dve.tensor_scalar(out_, x, c0, c1, op0, op1))

            dve.wait_ge(trig_act, 1)
            dve.tensor_tensor(Q[0], lr, dt_[:, :], mul).then_inc(trig, 1)
            tt(Q[1], li, dt_[:, :], mul)
            ts(Q[2], Q[1], 1.0 / (2 * PI), ROUND, mul, add)
            ts(Q[2], Q[2], ROUND, None, sub)
            for part in TWO_PI:
                own.then(dve.scalar_tensor_tensor(out=Q[1], in0=Q[2], scalar=-part, in1=Q[1], op0=mul, op1=add))
            ts(Q[1], Q[1], 3.1415925, -3.1415925, ALU.min, ALU.max)
            ts(Q[6], Q[1], -1.0, None, mul)
            tt(Q[6], Q[6], Q[1], ALU.max)
            dve.tensor_scalar(Q[2], Q[6], -1.0, PI / 2, mul, add).then_inc(trig, 1)
            dve.wait_ge(trig_act, 4)
            tt(pw[:, 0, 1, :], Q[3], Q[5], mul)
            tt(pw[:, 1, 1, :], Q[3], Q[4], mul)
            own.then(dve.memset(pw[:, 0, 0, :], 1.0))
            own.then(dve.memset(pw[:, 1, 0, :], 0.0))

            def cmul(dst, x, y, t0, t1):
                tt(t0, x[0], y[0], mul)
                tt(t1, x[1], y[1], mul)
                tt(dst[0], t0, t1, sub)
                tt(t0, x[0], y[1], mul)
                tt(t1, x[1], y[0], mul)
                tt(dst[1], t0, t1, add)

            for half in (1, 2, 4):
                src = [pw[:, part, 1:half + 1, :] for part in range(2)]
                by = [pw[:, part, half:half + 1, :].to_broadcast([P, half, KP]) for part in range(2)]
                dst = [pw[:, part, half + 1:2 * half + 1, :] for part in range(2)]
                t0, t1 = (tmp[:, x, 0:half * KP].rearrange("p (d k) -> p d k", k=KP) for x in range(2))
                cmul(dst, src, by, t0, t1)
            for j in range(J):
                own.then(dve.tensor_copy(pv[:, :, j, :], pw[:, :, J - 1 - j, :]))
            tt(Q[0], lr, lr, mul)
            tt(Q[1], li, li, mul)
            tt(Q[0], Q[0], Q[1], add)
            own.then(dve.reciprocal(Q[0], Q[0]))
            ts(Q[1], pw[:, 0, 1, :], 1.0, None, sub)
            ai = pw[:, 1, 1, :]
            tt(Q[2], Q[1], lr, mul)
            tt(Q[3], ai, li, mul)
            tt(Q[2], Q[2], Q[3], add)
            tt(Q[2], Q[2], Q[0], mul)
            tt(Q[3], ai, lr, mul)
            tt(Q[4], Q[1], li, mul)
            tt(Q[3], Q[3], Q[4], sub)
            tt(Q[3], Q[3], Q[0], mul)
            dve.wait_ge(b_loaded, 32)
            wide = [x.rearrange("p (k o) -> p k o", o=1).to_broadcast([P, KP, H]) for x in (Q[2], Q[3])]
            t0, t1 = (tmp[:, x, 0:KP * H].rearrange("p (k h) -> p k h", h=H) for x in range(2))
            cmul([b_bar[:, part, :, :] for part in range(2)], [b_in[:, part, :, :] for part in range(2)], wide, t0, t1)
            dve.wait_ge(x_kept_done, 16)
            dve.memset(toep[:, :, :], 0.0).then_inc(toep_clear, 1)
            dve.wait_ge(ssm_full, 1)
            own.then(dve.tensor_copy(c_mat[:, :, :, :].rearrange("p r k h -> p (r k h)"), unit[C_][:, 0:2 * KP * H]))
            dve.sem_inc(unit_free[C_], 1)

            def scan_setup():
                for l in range(LEVELS):
                    if l == 0:
                        for part in range(2):
                            own.then(dve.tensor_copy(lv[:, 0, part, :], pw[:, part, 8, :]))
                    else:
                        prev = [lv[:, l - 1, part, :] for part in range(2)]
                        cmul([lv[:, l, part, :] for part in range(2)], prev, prev, Q[6], Q[7])
                ts(lv[:, :, 2, :], lv[:, :, 1, :], -1.0, None, mul)
                own.then(dve.memset(sc_a[:, :, :, :], 0.0))
                own.then(dve.memset(sc_b[:, :, :, :], 0.0))

            def batch(t):
                dve.wait_ge(ssm_full, 1 + 4 * t)
                four = "p d (t k) -> p t k d"
                powers = [pw[:, part, :, :].rearrange(four, k=4)[:, t, :, :] for part in range(2)]
                late = [pv[:, part, :, :].rearrange(four, k=4)[:, t, :, :] for part in range(2)]
                bb = [b_bar[:, part, :, :].rearrange("p (t k) h -> p t k h", k=4)[:, t, :, :] for part in range(2)]
                cc = [c_mat[:, part, :, :].rearrange("p (t k) h -> p t k h", k=4)[:, t, :, :] for part in range(2)]
                for part in range(2):
                    own.then(dve.tensor_copy(b_now[:, :, part, :], bb[part]))

                def product(dst, powers_, x, n, conjugate):
                    (pr, pi), (xr_, xi) = ([y.rearrange("p k (d o) -> p k d o", o=1).to_broadcast([P, 4, n, H])
                                            for y in powers_],
                                           [y.rearrange("p k (o h) -> p k o h", o=1).to_broadcast([P, 4, n, H]) for y in x])
                    t0, t1 = (tmp[:, y, 0:4 * n * H].rearrange("p (k d h) -> p k d h", k=4, h=H) for y in range(2))
                    tt(t0, pr, xr_, mul)
                    tt(t1, pi, xi, mul)
                    tt(dst[:, :, 0, :, :], t0, t1, sub)
                    tt(t0, pr, xi, mul)
                    tt(t1, pi, xr_, mul)
                    if conjugate:
                        own.then(dve.scalar_tensor_tensor(out=dst[:, :, 1, :, :], in0=t0, scalar=-1.0, in1=t1,
                                                          op0=mul, op1=sub))
                    else:
                        tt(dst[:, :, 1, :, :], t0, t1, add)

                product(ba, late, bb, J, False)
                product(ca, powers, cc, J + 1, True)
                dve.sem_inc(ba_ready, 1)
                if isinstance(t, int):
                    scan_setup()

                dve.wait_ge(ssm_full, 4 + 4 * t)
                own.then(dve.tensor_copy(
                    sc_a[:, :, :, PAD + 1:PAD + C].rearrange("p k r c -> p (k r) c"),
                    unit[C_][:, :].rearrange("p (n c) -> p n c", c=C)[:, :, 0:C - 1]))
                dve.sem_inc(unit_free[C_], 1)
                n = 0
                for pair in range(2):
                    for l in range(LEVELS):
                        src, dst = ((sc_a, sc_b), (sc_b, sc_a))[l % 2]
                        off = 1 << l
                        now, then = slice(PAD, PAD + C), slice(PAD - off, PAD + C - off)
                        for to, from_, x, plus in ((0, 0, 0, src), (1, 1, 0, src), (0, 1, 2, dst), (1, 0, 1, dst)):
                            for kk in (2 * pair, 2 * pair + 1):
                                by = lv[:, l, x, :].rearrange("p (t k) -> p t k", k=4)[:, t, kk:kk + 1]
                                if n >= 2:
                                    dve.wait_ge(scan_step, 4 * 4 * LEVELS * t + n - 1)
                                dve.scalar_tensor_tensor(
                                    out=dst[:, kk, to, now], in0=src[:, kk, from_, then], scalar=by,
                                    in1=plus[:, kk, to, now], op0=mul, op1=add).then_inc(scan_step, 1)
                                n += 1
                dve.wait_ge(scan_step, 4 * 4 * LEVELS * (t + 1))
                dve.sem_inc(scan_done, 1)

            batch(0)
            with dve.Fori(1, NT) as t:
                own.enter(t - 1, 2 + 12 + 1)
                batch(t)
            own.leave(NT - 1)

            dve.wait_ge(y_loaded, 16 * NT)
            for t in range(NT):
                dve.scalar_tensor_tensor(out=u_all[:, t, :], in0=u_all[:, t, :], scalar=vt[:, DS + t:DS + t + 1],
                                         in1=y_all[:, t, :], op0=mul, op1=add).then_inc(s_sum, 1)

            def s_low_part(t, before):
                dve.wait_ge(s_split, before + t + 1)
                dve.tensor_tensor(s_low[:, t, :], u_all[:, t, :], s_high[:, t, :].bitcast(F32), sub).then_inc(s_ready, 1)

            for t in range(NT):
                s_low_part(t, 0)
            own.then(dve.memset(gv[:, 0:2, 0:1], 0.0))

            def conv_in(name, m0):
                here = at[name]
                with dve.Fori(0, 4) as m:
                    own.enter(m, 4)
                    dve.wait_ge(unit_free[A_], here.unit[A_] + m + 1)
                    dve.wait_ge(slab_used, here.slab + 3 * m + 2)
                    dve.tensor_tensor(gv[:, 2:, :].rearrange("p j c -> p (j c)"), s0[:, :], unit[B_][:, :],
                                      mul).then_inc(unit_free[B_], 1)
                    dve.wait_ge(unit_free[B_], here.unit[B_] + m + 1)
                    own.then(dve.tensor_copy(gv[:, 0:2, 1:C], gv[:, J:J + 2, 0:C - 1]))

                    def tap(k):
                        return column(vt[:, CW + k * KD + m0:CW + k * KD + m0 + 4], m)

                    def steps(j):
                        return gv[:, j:j + J, :].rearrange("p j c -> p (j c)")

                    own.then(dve.tensor_scalar(taps[:, :], steps(2), tap(2), None, mul))
                    for k in (1, 0):
                        own.then(dve.scalar_tensor_tensor(out=taps[:, :], in0=steps(k), scalar=tap(k),
                                                          in1=taps[:, :], op0=mul, op1=add))
                    dve.wait_ge(slab_used, here.slab + 3 * m + 3)
                    dve.tensor_tensor(za[:, m0:m0 + 4, :][:, m, :], taps[:, :], unit[C_][:, :],
                                      mul).then_inc(unit_free[C_], 1)
                    dve.wait_ge(unit_free[C_], here.unit[C_] + m + 1)
                own.leave(4)

            conv_in("conv_in0", 0)
            here = at["glu"]
            for t in range(NT):
                dve.wait_ge(unit_free[t], here.unit[t] + 1)
                dve.tensor_tensor(u_all[:, t, :], u_all[:, t, :], stage[t % 2][:, :], mul).then_inc(gated, 1)
            for t in range(NT):
                s_low_part(t, NT)
            conv_in("conv_in1", 4)

            here = at["ssm_out"]
            with dve.Fori(0, 2) as i:
                for u in range(4):
                    m = 4 * i + u
                    dve.wait_ge(h_split, here.h + m + 1)
                    dve.tensor_tensor(h_low[:, m, :], za[:, m, :], h_high[:, m, :].bitcast(F32), sub).then_inc(h_ready, 1)
                    dve.wait_ge(h_ready, here.h + m + 1)
                    dve.wait_ge(slab_used, here.slab + 2 * i + u // 2 + 1)
                    dve.wait_ge(sg_loaded[u % 2], 16 * (2 * i + u // 2 + 1))
                    dve.tensor_tensor(mb[:, m, :], stage[u % 2][:, :], unit[u][:, :], mul).then_inc(unit_free[u], 1)
            here = at["conv_out"]
            with dve.Fori(0, KD // 2) as i:
                for e in range(2):
                    m = 2 * i + e
                    dve.wait_ge(slab_used, here.slab + m + 1)
                    dve.wait_ge(sg_loaded[e], 16 * (4 + i + 1))
                    dve.tensor_tensor(merged[:, :], stage[e][:, :], unit[e][:, :], mul).then_inc(unit_free[e], 1)
                    dve.wait_ge(unit_free[e], here.unit[e] + i + 1)
                    dve.tensor_tensor(merged[:, :], merged[:, :], mb[:, m, :], add).then_inc(merged_done, 1)
                    dve.wait_ge(g_split, here.g + m + 1)
                    dve.tensor_tensor(g_low[:, m, :], merged[:, :], g_high[:, m, :].bitcast(F32), sub).then_inc(g_ready, 1)
                    dve.wait_ge(g_ready, here.g + m + 1)
            dve.wait_ge(x_back, 16 * KD)
            clear_sums(2)
            down("w_out", mod[:, GT[1]:GT[1] + KD], 2)
            norm(2, at["norm2"].h)
            for n in range(3):
                up("ffn2", n, False)
                if n == 2:
                    dve.wait_ge(g_ready, at["end"].g)
                    clear_sums(3)
                down(f"ffn2.down{n}", gate[1][:, :], 3 if n == 2 else None)
            dve.wait_ge(root_done, 7)
            dve.reciprocal(rms[:, :], rms[:, :]).then_inc(rms_ready, 1)
            dve.wait_ge(rms_ready, 1)
            dve.wait_ge(unit_free[A_], at["end"].unit[A_] + 4)
            dve.wait_ge(unit_free[B_], at["end"].unit[B_] + 4)
            for j in range(J):
                if not by_act(j):
                    dve.tensor_scalar(o_out[:, j, :], o_rows[:, j, :], rms[:, j:j + 1], None, mul).then_inc(o_final_dve, 1)


_INS = ['x', 'c', 'w_ada', 'b_ada', 'g_ffn1', 'w1_a', 'w3_a', 'w2_a', 'g_mix', 'w_in', 'conv_w', 'w_conv_out',
        'a_re', 'a_im', 'b_re', 'b_im', 'c_re', 'c_im', 'log_dt', 'd_skip', 'w_glu', 'w_ssm_out', 'w_out',
        'g_ffn2', 'w1_b', 'w3_b', 'w2_b', 'g_final']


def kernel(**inputs):
    import numpy as _np
    import concourse.bacc as _bacc
    from concourse import mybir as _mybir
    from concourse.bass_utils import run_bass_kernel_spmd as _run

    nc = _bacc.Bacc("TRN2", target_bir_lowering=False, num_devices=1, dynamic_dma_scratch_size=1024)
    arrays, args = {}, {}
    for name in _INS:
        v = _np.ascontiguousarray(inputs[name])
        arrays[f"in_{name}"] = v
        args[name] = nc.dram_tensor(f"in_{name}", v.shape, _mybir.dt.from_np(v.dtype), kind="ExternalInput").ap()
    out = nc.dram_tensor("out", (1, T, D), _mybir.dt.float32, kind="ExternalOutput").ap()
    block_kernel(nc, args, out)
    r = _run(nc, [arrays], core_ids=[0])
    return r.results[0]["out"]
```
